# Optimizing a Trainium2 kernel written in Bass

```python
import math
import jax, jax.numpy as jnp
from jax import lax
import numpy as np

D_MODEL = 1024
BATCH = 1
SEQ = 256
DEPTH = 2

D_FF = 2816
NORM_EPS = 1e-6
NSA_HEADS = 8
NSA_KV_HEADS = 2
NSA_GROUP = NSA_HEADS // NSA_KV_HEADS
NSA_HEAD_DIM = 64
CMP_BLOCK = 32
CMP_STRIDE = 16
SEL_BLOCK = 64
SEL_TOPK = 16
WINDOW = 512
Q_BLOCK = 128
ROPE_THETA = 10000.0
FORCE_SCORE = 1e4
SSD_HEADS = 16
SSD_HEAD_DIM = 64
SSD_D_INNER = SSD_HEADS * SSD_HEAD_DIM
SSD_GROUPS = 2
SSD_STATE = 128
SSD_CONV = 4
SSD_CHUNK = 128
SSD_NORM_EPS = 1e-5
RWKV_HEAD_DIM = 64
RWKV_HEADS = D_MODEL // RWKV_HEAD_DIM
DECAY_LORA = 64
AAA_LORA = 64
GATE_LORA = 160
RWKV_GN_EPS = 64e-5

N_EVEN = (DEPTH + 1) // 2
N_ODD = DEPTH // 2

NSA_Q_W = NSA_HEADS * NSA_HEAD_DIM
NSA_KV_W = NSA_KV_HEADS * NSA_HEAD_DIM
SSD_XBC = SSD_D_INNER + 2 * SSD_GROUPS * SSD_STATE
IN_SPLITS = (NSA_Q_W, NSA_KV_W, NSA_KV_W, NSA_KV_W, NSA_KV_W, NSA_KV_W, NSA_KV_W,
             NSA_HEADS * 3, SSD_D_INNER, SSD_XBC, SSD_HEADS)
IN_WIDTH = sum(IN_SPLITS)
MIX_OUT_WIDTH = NSA_Q_W + SSD_D_INNER


def rmsnorm(x, g, eps=NORM_EPS):
    xf = x.astype(jnp.float32)
    y = xf * lax.rsqrt(jnp.mean(xf * xf, -1, keepdims=True) + eps)
    return (y * g.astype(jnp.float32)).astype(x.dtype)

def swiglu(x, w_gate, w_up, w_down):
    return (jax.nn.silu(x @ w_gate) * (x @ w_up)) @ w_down

def rope_tables(seq, dim):
    inv = ROPE_THETA ** (-jnp.arange(0, dim, 2, dtype=jnp.float32) / dim)
    ang = jnp.arange(seq, dtype=jnp.float32)[:, None] * inv[None, :]
    return jnp.cos(ang), jnp.sin(ang)

def apply_rope(x, cos, sin):
    shape = (1, x.shape[1]) + (1,) * (x.ndim - 3) + (cos.shape[-1],)
    c = cos.reshape(shape).astype(x.dtype)
    s = sin.reshape(shape).astype(x.dtype)
    x1, x2 = jnp.split(x, 2, axis=-1)
    return jnp.concatenate([x1 * c - x2 * s, x2 * c + x1 * s], -1)

def masked_softmax(s, mask):
    s = jnp.where(mask, s.astype(jnp.float32), -1e30)
    p = jnp.where(mask, jnp.exp(s - jnp.max(s, -1, keepdims=True)), 0.0)
    return p / jnp.maximum(jnp.sum(p, -1, keepdims=True), 1e-30)

def compress_blocks(k, pe, w1, w2):
    b, s, h, d = k.shape
    n_cmp = (s - CMP_BLOCK) // CMP_STRIDE + 1
    idx = jnp.arange(n_cmp)[:, None] * CMP_STRIDE + jnp.arange(CMP_BLOCK)[None, :]
    blk = k[:, idx] + pe[None, None, :, None, :]
    blk = jnp.moveaxis(blk, 3, 2).reshape(b, n_cmp, h, CMP_BLOCK * d)
    return jax.nn.silu(blk @ w1) @ w2

def nsa_attention(q, k_cmp, v_cmp, k_sel, v_sel, k_win, v_win, gates,
                  pe_k, w1_k, w2_k, pe_v, w1_v, w2_v):
    b, s, hkv, g, d = q.shape
    kc = compress_blocks(k_cmp, pe_k, w1_k, w2_k)
    vc = compress_blocks(v_cmp, pe_v, w1_v, w2_v)
    n_cmp = kc.shape[1]
    n_sel = s // SEL_BLOCK
    topk = min(SEL_TOPK, n_sel)
    cmp_start = jnp.arange(n_cmp) * CMP_STRIDE
    cmp_end = cmp_start + CMP_BLOCK - 1
    sel_start = jnp.arange(n_sel) * SEL_BLOCK
    overlap = ((cmp_start[:, None] < sel_start[None, :] + SEL_BLOCK)
               & (cmp_end[:, None] >= sel_start[None, :])).astype(jnp.float32)
    ks_blk = jnp.moveaxis(k_sel, 2, 1).reshape(b, hkv, n_sel, SEL_BLOCK, d)
    vs_blk = jnp.moveaxis(v_sel, 2, 1).reshape(b, hkv, n_sel, SEL_BLOCK, d)
    pad = ((0, 0), (WINDOW, 0), (0, 0), (0, 0))
    kw_pad = jnp.pad(k_win, pad)
    vw_pad = jnp.pad(v_win, pad)
    bi = jnp.arange(b)[:, None, None, None]
    hi = jnp.arange(hkv)[None, :, None, None]
    blk_ids = jnp.arange(n_sel)

    def block(qi):
        s0 = qi * Q_BLOCK
        qb = lax.dynamic_slice_in_dim(q, s0, Q_BLOCK, 1)
        gb = lax.dynamic_slice_in_dim(gates, s0, Q_BLOCK, 1)
        t = s0 + jnp.arange(Q_BLOCK)
        p_c = masked_softmax(jnp.einsum('bqhgd,bchd->bhgqc', qb, kc),
                             cmp_end[None, :] <= t[:, None])
        o_c = jnp.einsum('bhgqc,bchd->bqhgd', p_c.astype(vc.dtype), vc)
        imp = jnp.einsum('bhgqc,cj->bhqj', p_c, overlap)
        cur = t // SEL_BLOCK
        forced = ((blk_ids[None, :] == 0) | (blk_ids[None, :] == cur[:, None])
                  | (blk_ids[None, :] == cur[:, None] - 1))
        valid = sel_start[None, :] <= t[:, None]
        imp = jnp.where(valid, jnp.where(forced, FORCE_SCORE, imp), -jnp.inf)
        _, sel = lax.top_k(imp, topk)
        kg = ks_blk[bi, hi, sel].reshape(b, hkv, Q_BLOCK, topk * SEL_BLOCK, d)
        vg = vs_blk[bi, hi, sel].reshape(b, hkv, Q_BLOCK, topk * SEL_BLOCK, d)
        tok = (sel[..., None] * SEL_BLOCK + jnp.arange(SEL_BLOCK)).reshape(
            b, hkv, Q_BLOCK, topk * SEL_BLOCK)
        p_s = masked_softmax(jnp.einsum('bqhgd,bhqnd->bhgqn', qb, kg),
                             (tok <= t[:, None])[:, :, None])
        o_s = jnp.einsum('bhgqn,bhqnd->bqhgd', p_s.astype(vg.dtype), vg)
        kw = lax.dynamic_slice_in_dim(kw_pad, s0, Q_BLOCK + WINDOW, 1)
        vw = lax.dynamic_slice_in_dim(vw_pad, s0, Q_BLOCK + WINDOW, 1)
        kp = s0 - WINDOW + jnp.arange(Q_BLOCK + WINDOW)
        mask_w = ((kp[None, :] <= t[:, None]) & (kp[None, :] > t[:, None] - WINDOW)
                  & (kp[None, :] >= 0))
        p_w = masked_softmax(jnp.einsum('bqhgd,bkhd->bhgqk', qb, kw), mask_w)
        o_w = jnp.einsum('bhgqk,bkhd->bqhgd', p_w.astype(vw.dtype), vw)
        return gb[..., 0:1] * o_c + gb[..., 1:2] * o_s + gb[..., 2:3] * o_w

    out = lax.map(block, jnp.arange(s // Q_BLOCK))
    return jnp.moveaxis(out, 0, 1).reshape(b, s, hkv * g * d)

def causal_depthwise_conv(x, w, bias):
    y = lax.conv_general_dilated(x, w, window_strides=(1,), padding=[(SSD_CONV - 1, 0)],
                                 dimension_numbers=('NWC', 'WIO', 'NWC'),
                                 feature_group_count=x.shape[-1])
    return y + bias

def ssd_chunked(x, dt, a, bmat, cmat):
    b, s, h, p = x.shape
    g, n = bmat.shape[2], bmat.shape[3]
    r = h // g
    l = SSD_CHUNK
    c = s // l
    xd = (x * dt[..., None]).reshape(b, c, l, g, r, p)
    a_cs = jnp.cumsum(jnp.moveaxis((dt * a).reshape(b, c, l, g, r), 2, -1), axis=-1)
    bm = bmat.reshape(b, c, l, g, n)
    cm = cmat.reshape(b, c, l, g, n)
    causal = jnp.tril(jnp.ones((l, l), bool))
    seg = jnp.exp(jnp.where(causal, a_cs[..., :, None] - a_cs[..., None, :], -jnp.inf))
    cb = jnp.einsum('bclgn,bcsgn->bcgls', cm, bm)
    y_diag = jnp.einsum('bcgrls,bcsgrp->bclgrp', cb[:, :, :, None] * seg, xd)
    decay_states = jnp.exp(a_cs[..., -1:] - a_cs)
    states = jnp.einsum('bclgn,bcgrl,bclgrp->bcgrpn', bm, decay_states, xd)
    chunk_decay = jnp.exp(a_cs[..., -1])

    def step(carry, inp):
        st, dec = inp
        return carry * dec[..., None, None] + st, carry

    _, states_in = lax.scan(step, jnp.zeros_like(states[:, 0]),
                            (jnp.moveaxis(states, 1, 0), jnp.moveaxis(chunk_decay, 1, 0)))
    states_in = jnp.moveaxis(states_in, 0, 1)
    y_off = jnp.einsum('bclgn,bcgrpn,bcgrl->bclgrp', cm, states_in, jnp.exp(a_cs))
    return (y_diag + y_off).reshape(b, s, h, p)

def mamba2_branch(z, xbc, dt_raw, conv_w, conv_b, dt_bias, a_log, d_skip, norm_w):
    b, s, _ = z.shape
    f32 = jnp.float32
    xbc = jax.nn.silu(causal_depthwise_conv(xbc, conv_w, conv_b))
    xs, bm, cm = jnp.split(xbc, [SSD_D_INNER, SSD_D_INNER + SSD_GROUPS * SSD_STATE], -1)
    xs = xs.reshape(b, s, SSD_HEADS, SSD_HEAD_DIM).astype(f32)
    dt = jax.nn.softplus(dt_raw.astype(f32) + dt_bias.astype(f32))
    a = -jnp.exp(a_log.astype(f32))
    y = ssd_chunked(xs, dt, a, bm.reshape(b, s, SSD_GROUPS, SSD_STATE).astype(f32),
                    cm.reshape(b, s, SSD_GROUPS, SSD_STATE).astype(f32))
    y = y + xs * d_skip.astype(f32)[:, None]
    y = y.reshape(b, s, SSD_D_INNER) * jax.nn.silu(z.astype(f32))
    yg = y.reshape(b, s, SSD_GROUPS, SSD_D_INNER // SSD_GROUPS)
    yg = yg * lax.rsqrt(jnp.mean(yg * yg, -1, keepdims=True) + SSD_NORM_EPS)
    return (yg.reshape(b, s, SSD_D_INNER) * norm_w.astype(f32)).astype(z.dtype)

def nsa_ssd_mixer(h, cos, sin, w_in, pe_k, w1_k, w2_k, pe_v, w1_v, w2_v,
                  conv_w, conv_b, dt_bias, a_log, d_skip, ssd_norm_w, w_out):
    b, s, _ = h.shape
    proj = h @ w_in
    offs = np.cumsum(IN_SPLITS)[:-1].tolist()
    q, kc, vc, ks, vs, kw, vw, gl, z, xbc, dt = jnp.split(proj, offs, -1)
    kvshape = (b, s, NSA_KV_HEADS, NSA_HEAD_DIM)
    q = apply_rope(q.reshape(b, s, NSA_KV_HEADS, NSA_GROUP, NSA_HEAD_DIM), cos, sin) * (NSA_HEAD_DIM ** -0.5)
    kc = apply_rope(kc.reshape(kvshape), cos, sin)
    ks = apply_rope(ks.reshape(kvshape), cos, sin)
    kw = apply_rope(kw.reshape(kvshape), cos, sin)
    gates = jax.nn.sigmoid(gl).reshape(b, s, NSA_KV_HEADS, NSA_GROUP, 3)
    o_a = nsa_attention(q, kc, vc.reshape(kvshape), ks, vs.reshape(kvshape), kw, vw.reshape(kvshape),
                        gates, pe_k, w1_k, w2_k, pe_v, w1_v, w2_v)
    o_b = mamba2_branch(z, xbc, dt, conv_w, conv_b, dt_bias, a_log, d_skip, ssd_norm_w)
    return jnp.concatenate([o_a, o_b], -1) @ w_out

def rwkv7_time_mix(h, mu, w_r, w_k, w_v, w_o, w0, w1, w2, a0, a1, a2, g1, g2,
                   k_k, k_a, r_k, ln_g, ln_b):
    b, s, d = h.shape
    f32 = jnp.float32
    xx = jnp.pad(h, ((0, 0), (1, 0), (0, 0)))[:, :-1] - h
    xr, xw, xk, xv, xa, xg = [h + xx * mu[i] for i in range(6)]
    r = xr @ w_r
    w = -jax.nn.softplus(-(w0 + jnp.tanh(xw @ w1) @ w2)) - 0.5
    k = xk @ w_k
    v = xv @ w_v
    a = jax.nn.sigmoid(a0 + (xa @ a1) @ a2)
    g = jax.nn.sigmoid(xg @ g1) @ g2
    heads = lambda t: t.reshape(b, s, RWKV_HEADS, RWKV_HEAD_DIM).astype(f32)
    kk = heads(k * k_k)
    kk = kk / jnp.maximum(jnp.sqrt(jnp.sum(kk * kk, -1, keepdims=True)), 1e-12)
    k = k * (1 + (a - 1) * k_a)
    r_, k_, v_, a_ = heads(r), heads(k), heads(v), heads(a)
    decay = jnp.exp(-jnp.exp(heads(w)))

    def step(state, inp):
        r_t, d_t, k_t, v_t, kk_t, a_t = inp
        sa = jnp.einsum('bhij,bhj->bhi', state, -kk_t)
        state = (state * d_t[:, :, None, :] + sa[..., None] * (kk_t * a_t)[:, :, None, :]
                 + v_t[..., None] * k_t[:, :, None, :])
        return state, jnp.einsum('bhij,bhj->bhi', state, r_t)

    xs = tuple(jnp.moveaxis(t, 1, 0) for t in (r_, decay, k_, v_, kk, a_))
    _, y = lax.scan(step, jnp.zeros((b, RWKV_HEADS, RWKV_HEAD_DIM, RWKV_HEAD_DIM), f32), xs)
    y = jnp.moveaxis(y, 0, 1)
    mean = jnp.mean(y, -1, keepdims=True)
    var = jnp.mean(jnp.square(y - mean), -1, keepdims=True)
    y = ((y - mean) * lax.rsqrt(var + RWKV_GN_EPS)).reshape(b, s, d)
    y = y * ln_g.astype(f32) + ln_b.astype(f32)
    bonus = jnp.sum(r_ * k_ * r_k.astype(f32), -1, keepdims=True) * v_
    y = y + bonus.reshape(b, s, d)
    return (y * g.astype(f32)).astype(h.dtype) @ w_o

def first_inputs(seed: int = 0) -> dict:
    key = jax.random.key(seed)
    ks = iter(jax.random.split(key, 48))
    nrm = lambda shape, scale: scale * jax.random.normal(next(ks), shape, jnp.float32)
    uni = lambda shape, lo, hi: jax.random.uniform(next(ks), shape, jnp.float32, lo, hi)
    D, F, E, O = D_MODEL, D_FF, N_EVEN, N_ODD
    L, KD = CMP_BLOCK, NSA_HEAD_DIM
    x = nrm((BATCH, SEQ, D), 1.0)
    norm_gains = 1.0 + nrm((DEPTH, 6, D), 0.05)
    ffn1_w_gate = nrm((DEPTH, D, F), D ** -0.5)
    ffn1_w_up = nrm((DEPTH, D, F), D ** -0.5)
    ffn1_w_down = nrm((DEPTH, F, D), F ** -0.5)
    ffn2_w_gate = nrm((DEPTH, D, F), D ** -0.5)
    ffn2_w_up = nrm((DEPTH, D, F), D ** -0.5)
    ffn2_w_down = nrm((DEPTH, F, D), F ** -0.5)
    ab_w_in = nrm((E, D, IN_WIDTH), D ** -0.5)
    a_cmp_pe_k = nrm((E, L, KD), 0.02)
    a_cmp_w1_k = nrm((E, L * KD, KD), (L * KD) ** -0.5)
    a_cmp_w2_k = nrm((E, KD, KD), KD ** -0.5)
    a_cmp_pe_v = nrm((E, L, KD), 0.02)
    a_cmp_w1_v = nrm((E, L * KD, KD), (L * KD) ** -0.5)
    a_cmp_w2_v = nrm((E, KD, KD), KD ** -0.5)
    b_conv_w = nrm((E, SSD_CONV, 1, SSD_XBC), SSD_CONV ** -0.5)
    b_conv_b = nrm((E, SSD_XBC), 0.02)
    dt0 = jnp.exp(uni((E, SSD_HEADS), math.log(1e-3), math.log(1e-1)))
    b_dt_bias = dt0 + jnp.log(-jnp.expm1(-dt0))
    b_a_log = jnp.log(uni((E, SSD_HEADS), 1.0, 16.0))
    b_d_skip = 1.0 + nrm((E, SSD_HEADS), 0.1)
    b_norm_w = 1.0 + nrm((E, SSD_D_INNER), 0.05)
    ab_w_out = nrm((E, MIX_OUT_WIDTH, D), MIX_OUT_WIDTH ** -0.5)
    c_mu = uni((O, 6, D), 0.0, 1.0)
    c_w_r = nrm((O, D, D), D ** -0.5)
    c_w_k = nrm((O, D, D), D ** -0.5)
    c_w_v = nrm((O, D, D), D ** -0.5)
    c_w_o = nrm((O, D, D), D ** -0.5)
    c_w0 = uni((O, D), -6.0, 1.0)
    c_w1 = nrm((O, D, DECAY_LORA), D ** -0.5)
    c_w2 = nrm((O, DECAY_LORA, D), 0.1 * DECAY_LORA ** -0.5)
    c_a0 = nrm((O, D), 0.1)
    c_a1 = nrm((O, D, AAA_LORA), D ** -0.5)
    c_a2 = nrm((O, AAA_LORA, D), 0.1 * AAA_LORA ** -0.5)
    c_g1 = nrm((O, D, GATE_LORA), D ** -0.5)
    c_g2 = nrm((O, GATE_LORA, D), GATE_LORA ** -0.5)
    c_k_k = 0.85 + nrm((O, D), 0.05)
    c_k_a = 1.0 + nrm((O, D), 0.05)
    c_r_k = nrm((O, RWKV_HEADS, RWKV_HEAD_DIM), 0.1)
    c_ln_g = 1.0 + nrm((O, D), 0.05)
    c_ln_b = nrm((O, D), 0.02)
    return {'x': x, 'norm_gains': norm_gains,
            'ffn1_w_gate': ffn1_w_gate, 'ffn1_w_up': ffn1_w_up, 'ffn1_w_down': ffn1_w_down,
            'ffn2_w_gate': ffn2_w_gate, 'ffn2_w_up': ffn2_w_up, 'ffn2_w_down': ffn2_w_down,
            'ab_w_in': ab_w_in, 'a_cmp_pe_k': a_cmp_pe_k, 'a_cmp_w1_k': a_cmp_w1_k,
            'a_cmp_w2_k': a_cmp_w2_k, 'a_cmp_pe_v': a_cmp_pe_v, 'a_cmp_w1_v': a_cmp_w1_v,
            'a_cmp_w2_v': a_cmp_w2_v, 'b_conv_w': b_conv_w, 'b_conv_b': b_conv_b,
            'b_dt_bias': b_dt_bias, 'b_a_log': b_a_log, 'b_d_skip': b_d_skip,
            'b_norm_w': b_norm_w, 'ab_w_out': ab_w_out,
            'c_mu': c_mu, 'c_w_r': c_w_r, 'c_w_k': c_w_k, 'c_w_v': c_w_v, 'c_w_o': c_w_o,
            'c_w0': c_w0, 'c_w1': c_w1, 'c_w2': c_w2, 'c_a0': c_a0, 'c_a1': c_a1, 'c_a2': c_a2,
            'c_g1': c_g1, 'c_g2': c_g2, 'c_k_k': c_k_k, 'c_k_a': c_k_a, 'c_r_k': c_r_k,
            'c_ln_g': c_ln_g, 'c_ln_b': c_ln_b}

def first_block(x, norm_gains, ffn1_w_gate, ffn1_w_up, ffn1_w_down, ffn2_w_gate, ffn2_w_up,
              ffn2_w_down, ab_w_in, a_cmp_pe_k, a_cmp_w1_k, a_cmp_w2_k, a_cmp_pe_v, a_cmp_w1_v,
              a_cmp_w2_v, b_conv_w, b_conv_b, b_dt_bias, b_a_log, b_d_skip, b_norm_w, ab_w_out,
              c_mu, c_w_r, c_w_k, c_w_v, c_w_o, c_w0, c_w1, c_w2, c_a0, c_a1, c_a2, c_g1, c_g2,
              c_k_k, c_k_a, c_r_k, c_ln_g, c_ln_b):
    cos, sin = rope_tables(x.shape[1], NSA_HEAD_DIM)
    for layer in range(DEPTH):
        ng = norm_gains[layer]
        hdn = swiglu(rmsnorm(x, ng[0]), ffn1_w_gate[layer], ffn1_w_up[layer], ffn1_w_down[layer])
        x = x + 0.5 * rmsnorm(hdn, ng[1])
        hdn = rmsnorm(x, ng[2])
        i = layer // 2
        if layer % 2 == 0:
            hdn = nsa_ssd_mixer(hdn, cos, sin, ab_w_in[i], a_cmp_pe_k[i], a_cmp_w1_k[i],
                                a_cmp_w2_k[i], a_cmp_pe_v[i], a_cmp_w1_v[i], a_cmp_w2_v[i],
                                b_conv_w[i], b_conv_b[i], b_dt_bias[i], b_a_log[i], b_d_skip[i],
                                b_norm_w[i], ab_w_out[i])
        else:
            hdn = rwkv7_time_mix(hdn, c_mu[i], c_w_r[i], c_w_k[i], c_w_v[i], c_w_o[i], c_w0[i],
                                 c_w1[i], c_w2[i], c_a0[i], c_a1[i], c_a2[i], c_g1[i], c_g2[i],
                                 c_k_k[i], c_k_a[i], c_r_k[i], c_ln_g[i], c_ln_b[i])
        x = x + rmsnorm(hdn, ng[3])
        hdn = swiglu(rmsnorm(x, ng[4]), ffn2_w_gate[layer], ffn2_w_up[layer], ffn2_w_down[layer])
        x = x + 0.5 * rmsnorm(hdn, ng[5])
    return x


N_META = 16
MIX_WIDTH = D_MODEL
DIFF_WIDTH = MIX_WIDTH // 2
FOX_WIDTH = MIX_WIDTH - DIFF_WIDTH
DIFF_QK_DIM = 64
DIFF_V_DIM = 2 * DIFF_QK_DIM
DIFF_HEADS = DIFF_WIDTH // DIFF_V_DIM
FOX_HEAD_DIM = 64
FOX_HEADS = FOX_WIDTH // FOX_HEAD_DIM
SPLITS = (DIFF_HEADS * 2 * DIFF_QK_DIM, DIFF_HEADS * 2 * DIFF_QK_DIM, DIFF_WIDTH, DIFF_WIDTH,
          FOX_WIDTH, FOX_WIDTH, FOX_WIDTH, FOX_WIDTH, FOX_HEADS)
PROJ_WIDTH = sum(SPLITS)


def rms_norm(x, g):
    xf = x.astype(jnp.float32)
    y = xf * lax.rsqrt(jnp.mean(xf * xf, axis=-1, keepdims=True) + NORM_EPS)
    return (y * g.astype(jnp.float32)).astype(x.dtype)

def rope(t, pos):
    half = t.shape[-1] // 2
    inv = ROPE_THETA ** (-jnp.arange(half, dtype=jnp.float32) / half)
    ang = pos.astype(jnp.float32)[:, None] * inv[None, :]
    cos, sin = jnp.cos(ang), jnp.sin(ang)
    tf = t.astype(jnp.float32)
    t1, t2 = tf[..., :half], tf[..., half:]
    return jnp.concatenate([t1 * cos - t2 * sin, t2 * cos + t1 * sin], axis=-1).astype(t.dtype)

def sweep_query_blocks(block_fn, q_parts, pos):
    meta_out = block_fn(tuple(q[:, :, :N_META] for q in q_parts), pos[:N_META])

    def to_blocks(q):
        b, h, _, d = q.shape
        return jnp.moveaxis(q[:, :, N_META:].reshape(b, h, -1, Q_BLOCK, d), 2, 0)

    blocks = tuple(to_blocks(q) for q in q_parts)
    pos_blocks = pos[N_META:].reshape(-1, Q_BLOCK)
    outs = lax.map(lambda a: block_fn(a[0], a[1]), (blocks, pos_blocks))
    nb, b, h, t, dv = outs.shape
    real = jnp.moveaxis(outs, 0, 2).reshape(b, h, nb * t, dv)
    return jnp.concatenate([meta_out, real], axis=2)

def hybrid_layer(h, pos, norm_g, w_in, b_forget, lam_q1, lam_k1, lam_q2, lam_k2,
                 subln_g, w_out, lambda_init):
    bsz, length, _ = h.shape
    u = rms_norm(h, norm_g)
    proj = jnp.einsum('bld,dp->blp', u, w_in)
    split_points = np.cumsum(SPLITS)[:-1].tolist()
    dq, dk, dv, dz, fq, fk, fv, fz, f_logit = jnp.split(proj, split_points, axis=-1)

    def diff_qk(t):
        t = t.reshape(bsz, length, DIFF_HEADS, 2, DIFF_QK_DIM).transpose(3, 0, 2, 1, 4)
        return rope(t[0], pos), rope(t[1], pos)

    q1, q2 = diff_qk(dq)
    k1, k2 = diff_qk(dk)
    v_a = dv.reshape(bsz, length, DIFF_HEADS, DIFF_V_DIM).transpose(0, 2, 1, 3)
    lam = (jnp.exp(jnp.sum(lam_q1.astype(jnp.float32) * lam_k1.astype(jnp.float32)))
           - jnp.exp(jnp.sum(lam_q2.astype(jnp.float32) * lam_k2.astype(jnp.float32)))
           + lambda_init)
    d_scale = DIFF_QK_DIM ** -0.5

    def diff_block(qs, qpos):
        qa, qc = qs
        mask = pos[None, :] <= qpos[:, None]

        def probs(q, k):
            s = jnp.einsum('bhqd,bhkd->bhqk', q, k).astype(jnp.float32) * d_scale
            return jax.nn.softmax(jnp.where(mask, s, -jnp.inf), axis=-1)

        p = probs(qa, k1) - lam * probs(qc, k2)
        return jnp.einsum('bhqk,bhkd->bhqd', p.astype(v_a.dtype), v_a)

    o_a = sweep_query_blocks(diff_block, (q1, q2), pos)
    o_a = rms_norm(o_a, subln_g.reshape(DIFF_HEADS, 1, DIFF_V_DIM)) * (1.0 - lambda_init)
    o_a = o_a.transpose(0, 2, 1, 3).reshape(bsz, length, DIFF_WIDTH)

    def fox_heads(t):
        return t.reshape(bsz, length, FOX_HEADS, FOX_HEAD_DIM).transpose(0, 2, 1, 3)

    q_f, k_f, v_f = fox_heads(fq), fox_heads(fk), fox_heads(fv)
    log_f = jax.nn.log_sigmoid(f_logit.astype(jnp.float32) + b_forget.astype(jnp.float32))
    cum = jnp.cumsum(log_f, axis=1).transpose(0, 2, 1)
    f_scale = FOX_HEAD_DIM ** -0.5

    def fox_block(qs, qpos):
        q, c_q = qs
        mask = pos[None, :] <= qpos[:, None]
        s = (jnp.einsum('bhqd,bhkd->bhqk', q, k_f).astype(jnp.float32) * f_scale
             + c_q - cum[:, :, None, :])
        p = jax.nn.softmax(jnp.where(mask, s, -jnp.inf), axis=-1)
        return jnp.einsum('bhqk,bhkd->bhqd', p.astype(v_f.dtype), v_f)

    o_b = sweep_query_blocks(fox_block, (q_f, cum[..., None]), pos)
    o_b = o_b.transpose(0, 2, 1, 3).reshape(bsz, length, FOX_WIDTH)

    mixed = jnp.concatenate([o_a * jax.nn.silu(dz), o_b * jax.nn.silu(fz)], axis=-1)
    return h + jnp.einsum('blm,md->bld', mixed, w_out)

def second_inputs(seed: int = 0) -> dict:
    key = jax.random.key(seed)
    ks = jax.random.split(key, 14)
    f32 = jnp.float32
    x = jax.random.normal(ks[0], (BATCH, SEQ, D_MODEL), f32)
    meta_tokens = jax.random.normal(ks[1], (N_META, D_MODEL), f32)
    norm_g = 1.0 + 0.02 * jax.random.normal(ks[2], (DEPTH, D_MODEL), f32)
    w_in = jax.random.normal(ks[3], (DEPTH, D_MODEL, PROJ_WIDTH), f32) * D_MODEL ** -0.5
    b_forget = (jnp.linspace(1.0, 6.0, FOX_HEADS, dtype=f32)[None, :]
                + 0.1 * jax.random.normal(ks[4], (DEPTH, FOX_HEADS), f32))
    lam_q1 = 0.1 * jax.random.normal(ks[5], (DEPTH, DIFF_QK_DIM), f32)
    lam_k1 = 0.1 * jax.random.normal(ks[6], (DEPTH, DIFF_QK_DIM), f32)
    lam_q2 = 0.1 * jax.random.normal(ks[7], (DEPTH, DIFF_QK_DIM), f32)
    lam_k2 = 0.1 * jax.random.normal(ks[8], (DEPTH, DIFF_QK_DIM), f32)
    subln_g = 1.0 + 0.02 * jax.random.normal(ks[9], (DEPTH, DIFF_WIDTH), f32)
    w_out = jax.random.normal(ks[10], (DEPTH, MIX_WIDTH, D_MODEL), f32) * MIX_WIDTH ** -0.5
    final_g = 1.0 + 0.02 * jax.random.normal(ks[11], (D_MODEL,), f32)
    return {'x': x, 'meta_tokens': meta_tokens, 'norm_g': norm_g, 'w_in': w_in,
            'b_forget': b_forget, 'lam_q1': lam_q1, 'lam_k1': lam_k1, 'lam_q2': lam_q2,
            'lam_k2': lam_k2, 'subln_g': subln_g, 'w_out': w_out, 'final_g': final_g}

def second_block(x, meta_tokens, norm_g, w_in, b_forget, lam_q1, lam_k1, lam_q2, lam_k2,
              subln_g, w_out, final_g):
    bsz, _, dm = x.shape
    meta = jnp.broadcast_to(meta_tokens.astype(x.dtype)[None], (bsz, N_META, dm))
    h = jnp.concatenate([meta, x], axis=1)
    pos = jnp.arange(h.shape[1], dtype=jnp.int32)
    for layer in range(DEPTH):
        lambda_init = 0.8 - 0.6 * math.exp(-0.3 * layer)
        h = hybrid_layer(h, pos, norm_g[layer], w_in[layer], b_forget[layer],
                         lam_q1[layer], lam_k1[layer], lam_q2[layer], lam_k2[layer],
                         subln_g[layer], w_out[layer], lambda_init)
    return rms_norm(h, final_g)[:, N_META:]


def setup_inputs(seed=0):
    out = dict(first_inputs(seed))
    for name, value in second_inputs(seed + 1).items():
        if name != "x":
            out[name + "_2"] = value
    return out


def reference(
    x, norm_gains, ffn1_w_gate, ffn1_w_up, ffn1_w_down, ffn2_w_gate, ffn2_w_up, ffn2_w_down,
    ab_w_in, a_cmp_pe_k, a_cmp_w1_k, a_cmp_w2_k, a_cmp_pe_v, a_cmp_w1_v, a_cmp_w2_v, b_conv_w,
    b_conv_b, b_dt_bias, b_a_log, b_d_skip, b_norm_w, ab_w_out, c_mu, c_w_r, c_w_k, c_w_v,
    c_w_o, c_w0, c_w1, c_w2, c_a0, c_a1, c_a2, c_g1, c_g2, c_k_k, c_k_a, c_r_k, c_ln_g, c_ln_b,
    meta_tokens_2, norm_g_2, w_in_2, b_forget_2, lam_q1_2, lam_k1_2, lam_q2_2, lam_k2_2,
    subln_g_2, w_out_2, final_g_2,
):
    x = first_block(
        x, norm_gains, ffn1_w_gate, ffn1_w_up, ffn1_w_down, ffn2_w_gate, ffn2_w_up, ffn2_w_down,
        ab_w_in, a_cmp_pe_k, a_cmp_w1_k, a_cmp_w2_k, a_cmp_pe_v, a_cmp_w1_v, a_cmp_w2_v,
        b_conv_w, b_conv_b, b_dt_bias, b_a_log, b_d_skip, b_norm_w, ab_w_out, c_mu, c_w_r,
        c_w_k, c_w_v, c_w_o, c_w0, c_w1, c_w2, c_a0, c_a1, c_a2, c_g1, c_g2, c_k_k, c_k_a,
        c_r_k, c_ln_g, c_ln_b,
    )
    return second_block(
        x, meta_tokens_2, norm_g_2, w_in_2, b_forget_2, lam_q1_2, lam_k1_2, lam_q2_2, lam_k2_2,
        subln_g_2, w_out_2, final_g_2,
    )


_drawn_inputs = setup_inputs


def setup_inputs(seed=0):
    import zlib

    import numpy as np

    out = dict(_drawn_inputs(seed))
    spreads = {}
    factors = {'a_cmp_pe_k': 8.0,
     'a_cmp_pe_v': 8.0,
     'c_w1': 8.0,
     'c_w2': 8.0,
     'c_ln_b': 3.984,
     'norm_g_2': 6.185,
     'lam_q2_2': 8.0,
     'subln_g_2': 8.0,
     'final_g_2': 2.672}
    for name, (base, spread) in spreads.items():
        noise = np.random.default_rng([zlib.crc32(name.encode()), seed]).standard_normal(out[name].shape)
        drawn = base * np.exp(spread * noise) if base else spread * noise
        out[name] = __import__('jax').numpy.asarray(drawn.astype(out[name].dtype))
    for name, factor in factors.items():
        out[name] = (out[name] * factor).astype(out[name].dtype)
    return out
```

```python
import numpy as np
import concourse.bass as bass
from concourse import mybir
from contextlib import ExitStack

F32 = mybir.dt.float32
ALU = mybir.AluOpType
ACT = mybir.ActivationFunctionType
AX = mybir.AxisListType.X

P = 128
S = 256
T = S // P
D = 1024
KD = D // P
F = 2816
NPAIR = F // (2 * P)
META = 16
L2 = META + S
SCR = 1.0 / 8.0
MASKED = -1e30
HD = 64
NH, NKV = 8, 2
NCMP = (S - 32) // 16 + 1
Q0, KC0, VC0, KS0, VS0, KW0, VW0, GL0, Z0, XBC0, DT0 = np.cumsum(
    [0, 512, 128, 128, 128, 128, 128, 128, 24, 1024, 1536]).tolist()
SH = 16
NSLOT = 6
SLOT = 2048

COLS_A = {"ng": 0, "conv_w": 48, "conv_b": 96, "ssd_norm": 108}
COLS_B = {"mu": 0, "w0": 48, "a0": 56, "k_k": 64, "k_a": 72, "r_k": 80, "norm_g2": 88}
NROW_A, NROW_B = 116, 104

CONST = {}
_at = 0
for _name, _n in (("ident", P), ("rot", P), ("blockones", P), ("ones", P), ("upper", P), ("strict", P), ("upper2", P),
                  ("qmask", L2), ("segmask", P), ("level", 7 * P), ("level1", P), ("cmpadd", T * NCMP),
                  ("cmpmul", T * NCMP), ("cos", L2), ("sin", L2), ("pairsel", 2), ("eps", 3)):
    CONST[_name] = (_at, _n)
    _at += _n
NCONST = _at


def constants():
    c = np.zeros((P, NCONST), np.float32)

    def put(name, a):
        o, n = CONST[name]
        c[:, o:o + n] = a

    i = np.arange(P)
    put("ident", np.eye(P))
    rot = np.zeros((P, P))
    for m in range(P):
        if m % 64 < 32:
            rot[m + 32, m] = -1
        else:
            rot[m - 32, m] = 1
    put("rot", rot)
    put("blockones", (i[:, None] // 64) == (i[None, :] // 64))
    put("ones", 1)
    put("upper", i[:, None] <= i[None, :])
    put("upper2", i[:, None] <= i[None, :])
    put("strict", i[:, None] < i[None, :])
    qm = np.zeros((P, L2))
    qm[:, L2 - P:] = np.where(i[None, :] <= i[:, None], 0, MASKED)
    put("qmask", qm)
    put("segmask", np.where(i[:, None] <= i[None, :], 0, MASKED))
    lv = []
    for n in (1, 2, 4, 8, 16, 32, 64):
        s, t = i[:, None], i[None, :]
        lv.append((s // (2 * n) == t // (2 * n)) & (s % (2 * n) < n) & (t % (2 * n) >= n))
    put("level", np.concatenate(lv, 1))
    put("level1", lv[0].T)
    tok = i[:, None, None] + P * np.arange(T)[None, :, None]
    ok = (np.arange(NCMP) * 16 + 31)[None, None, :] <= tok
    put("cmpadd", np.where(ok, 0, MASKED).reshape(P, -1))
    put("cmpmul", ok.reshape(P, -1))
    inv = np.float32(10000.0) ** (-np.arange(0, 64, 2, dtype=np.float32) / np.float32(64))
    ang = np.arange(L2, dtype=np.float32)[None, :] * inv[:, None]
    put("cos", np.tile(np.cos(ang), (4, 1)))
    put("sin", np.tile(np.sin(ang), (4, 1)))
    put("pairsel", (i[:, None] // 64) == np.arange(2)[None, :])
    put("eps", np.array([[1e-6, 1e-5, 64e-5]]))
    return c


class Turn:

    def __init__(self):
        self.n = 0

    def __call__(self):
        self.n += 1
        return self.n


class Arena:

    def __init__(self, base):
        self.base, self.top = base, 0

    def take(self, n, start=None):
        at = self.top if start is None else start
        self.top = max(self.top, at + n) if start is not None else at + n
        assert at + n <= self.base.shape[1], (at, n)
        return self.base[:, at:at + n]


def plan_weights(d):
    plan, at = [], {}

    def wide(w, c0, n=256):
        return (P, 0, (KD, n), w.rearrange("(k p) n -> p k n", p=P)[:, :, c0:c0 + n])

    def tall(w, k0, n=2):
        return (P, 0, (n, D), w.rearrange("(k p) n -> p k n", p=P)[:, k0:k0 + n, :])

    def ffn(key, g, u, dn):
        at[key] = len(plan)
        for q in range(NPAIR):
            plan.append([wide(g, 256 * q)])
            plan.append([wide(u, 256 * q)])
            plan.append([tall(dn, 2 * q)])

    for layer in range(2):
        ffn(("ffn", 2 * layer), d["ffn1_w_gate"][layer], d["ffn1_w_up"][layer], d["ffn1_w_down"][layer])
        if layer == 0:
            w = d["ab_w_in"][0]
            at["mixer"] = len(plan)
            for j in (0, 2):
                slot = []
                for jj in (0, 1):
                    for g in range(NKV):
                        c = Q0 + g * 256 + (j + jj) * HD
                        slot.append((P, (jj * P + g * HD, 256), (KD, HD),
                                     w.rearrange("(k p) n -> p k n", p=P)[:, :, c:c + HD]))
                plan.append(slot)
            plan.append([wide(w, KC0)])
            plan.append([wide(w, KS0)])
            plan.append([wide(w, KW0)])
            plan.append([(P, (0, 256), (KD, 24), w.rearrange("(k p) n -> p k n", p=P)[:, :, GL0:GL0 + 24]),
                         (P, (24, 256), (KD, 16), w.rearrange("(k p) n -> p k n", p=P)[:, :, DT0:DT0 + 16])])
            for c in range(4):
                plan.append([wide(w, Z0 + 256 * c)])
            for c in range(6):
                plan.append([wide(w, XBC0 + 256 * c)])
            for n in ("a_cmp_w1_k", "a_cmp_w1_v"):
                plan.append([(64, 0, (32, 64), d[n][0].rearrange("(l d) e -> d l e", d=64))])
            at["mixer_out"] = len(plan)
            for c in range(6):
                plan.append([tall(d["ab_w_out"][0], 2 * c)])
        else:
            at["rwkv"] = len(plan)
            for n in ("c_w_r", "c_w_k", "c_w_v"):
                for c in range(4):
                    plan.append([wide(d[n][0], 256 * c)])
            plan.append([(P, 0, (KD, 64), d["c_w1"][0].rearrange("(k p) n -> p k n", p=P)),
                         (P, 512, (KD, 64), d["c_a1"][0].rearrange("(k p) n -> p k n", p=P))])
            plan.append([(64, 0, (1, D), d["c_w2"][0].rearrange("p (o n) -> p o n", o=1)),
                         (64, D, (1, D), d["c_a2"][0].rearrange("p (o n) -> p o n", o=1))])
            plan.append([(P, 0, (KD, 160), d["c_g1"][0].rearrange("(k p) n -> p k n", p=P))])
            plan.append([(P, 0, (1, D), d["c_g2"][0][0:P, :].rearrange("p (o n) -> p o n", o=1)),
                         (32, D, (1, D), d["c_g2"][0][P:160, :].rearrange("p (o n) -> p o n", o=1))])
            at["rwkv_out"] = len(plan)
            for c in range(4):
                plan.append([tall(d["c_w_o"][0], 2 * c)])
        ffn(("ffn", 2 * layer + 1), d["ffn2_w_gate"][layer], d["ffn2_w_up"][layer], d["ffn2_w_down"][layer])
    for layer in range(2):
        at[("hybrid", layer)] = len(plan)
        for c in range(16):
            plan.append([wide(d["w_in_2"][layer], 256 * c)])
        plan.append([wide(d["w_in_2"][layer], 4096, 8)])
        at[("hybrid_out", layer)] = len(plan)
        for c in range(4):
            plan.append([tall(d["w_out_2"][layer], 2 * c)])
    return plan, at


def model_kernel(nc, d, out, stop=None):
    ctx = ExitStack()
    with ctx:
        def sb(name, shape):
            return ctx.enter_context(nc.sbuf_tensor(name, shape, F32))

        def sem(name):
            return ctx.enter_context(nc.semaphore(name))

        ring = sb("ring", [P, NSLOT, SLOT])
        x = sb("x", [P, T, D])
        xm = sb("xm", [META, D])
        hT = sb("hT", [P, KD, L2])
        gains = sb("gains", [P, 12, D])
        cst = sb("cst", [P, NCONST])
        colA = sb("colA", [P, NROW_A])
        colB = sb("colB", [P, NROW_B])
        small = sb("small", [P, 512])
        arena = sb("arena", [P, 18700])
        ps = ctx.enter_context(nc.psum_tensor("ps", [P, 8, 512], F32))

        def const(name, rows=P):
            o, n = CONST[name]
            return cst[0:rows, o:o + n]

        ident, ones = const("ident"), const("ones")
        qmask, level = const("qmask"), const("level")
        LN_G, LN_B, SUBLN, FINAL_G, LAMB = 6, 7, 8, 9, 10
        dt_bias, a_log, d_skip = small[:, 0:16], small[:, 16:32], small[:, 32:48]
        forget = small[0:8, 48:50]
        stat = small[:, 64:96]
        lam = small[:, 96:100]
        peT = [small[0:64, 128:160], small[0:64, 160:192]]
        w2k, w2v = small[0:64, 192:320], small[0:64, 320:384]

        first_in = sem("first_in")
        later_in = sem("later_in")
        slot_in = [sem(f"slot_in{i}") for i in range(NSLOT)]
        slot_used = sem("slot_used")
        stage_done = sem("stage_done")
        to_dve, dve_out = sem("to_dve"), sem("dve_out")
        to_act, act_out = sem("to_act"), sem("act_out")
        dve_step, act_step = sem("dve_step"), sem("act_step")
        gate_up, silu_done, hidden, down = sem("gate_up"), sem("silu_done"), sem("hidden"), sem("down")
        out_done = sem("out_done")

        plan, at = plan_weights(d)
        slot_value, total = [], [0] * NSLOT
        for n, parts in enumerate(plan):
            total[n % NSLOT] += 16 * len(parts)
            slot_value.append(total[n % NSLOT])

        n_first, n_later = Turn(), Turn()
        pe_d, pe_a, pe_sync = Turn(), Turn(), Turn()
        dve_d, dve_sync, dve_link = Turn(), Turn(), Turn()
        act_a, act_sync, act_link = Turn(), Turn(), Turn()

        def step_end(eng, turn):
            eng.drain().then_inc(stage_done, 1)
            eng.wait_ge(stage_done, 3 * turn())

        def pe_end(pe):
            step_end(pe, pe_sync)

        def dve_end(dve):
            step_end(dve, dve_sync)

        def act_end(act):
            step_end(act, act_sync)

        def dlink(dve, ins):
            ins.then_inc(dve_step, 1)
            dve.wait_ge(dve_step, dve_link())

        def alink(act, ins):
            ins.then_inc(act_step, 1)
            act.wait_ge(act_step, act_link())

        def group(o, pairs):
            for i, (l, r) in enumerate(pairs):
                last = nc.tensor.matmul(o, l, r, start=(i == 0), stop=(i == len(pairs) - 1))
            return last

        def bank_d(n):
            return ps[:, (n - 1) % 4, :]

        def bank_a(n):
            return ps[:, 4 + (n - 1) % 4, :]

        def slot8(n, w=256):
            return ring[:, n % NSLOT, 0:KD * w].rearrange("p (k n) -> p k n", k=KD)

        def slot2(n):
            return ring[:, n % NSLOT, :].rearrange("p (c n) -> p c n", c=2)

        def take_slot(pe, n):
            pe.wait_ge(slot_in[n % NSLOT], slot_value[n])

        def load_slot(sp, n):
            if n >= NSLOT:
                sp.wait_ge(slot_used, n - NSLOT + 1)
            for rows, first, (k, w), src in plan[n]:
                base = ring[0:rows, n % NSLOT, :]
                if isinstance(first, tuple):
                    dst = base.rearrange("p (k n) -> p k n", n=first[1])[:, :, first[0]:first[0] + w]
                else:
                    dst = base[:, first:first + k * w].rearrange("p (k n) -> p k n", k=k)
                sp.dma_start(dst, src).then_inc(slot_in[n % NSLOT], 16)

        def load_ffn(sp, call, g, u, dn):
            s0 = at[("ffn", call)]
            gv = g.rearrange("(k p) n -> p k n", p=P)
            uv = u.rearrange("(k p) n -> p k n", p=P)
            dv = dn.rearrange("(k p) n -> p k n", p=P)
            for n in range(s0, s0 + 6):
                load_slot(sp, n)
            with sp.Fori(1, NPAIR // 2) as i:
                for c in range(6):
                    n = s0 + c
                    q = c // 3
                    sp.wait_ge(slot_used, i * 6 + (n - NSLOT + 1))
                    dst = slot2(n) if c % 3 == 2 else slot8(n)
                    if c % 3 == 2:
                        src = dv[:, bass.ds(i * 4 + 2 * q, 2), :]
                    else:
                        src = (gv, uv)[c % 3][:, :, bass.ds(i * 512 + 256 * q, 256)]
                    sp.dma_start(dst, src).then_inc(slot_in[n % NSLOT], 16)
            for n in range(s0 + 6 * (NPAIR // 2), s0 + 3 * NPAIR):
                load_slot(sp, n)

        XN, XMN, SQ = arena[:, 0:2048], arena[0:META, 2048:3072], arena[:, 3072:4096]
        xn = XN.rearrange("p (t n) -> p t n", t=T)

        def root_act(act, cols, count, eps, rows=P):
            nc.scalar.activation(stat[0:rows, cols], stat[0:rows, cols], ACT.Sqrt, scale=1.0 / count,
                                 bias=const("eps", rows)[:, eps:eps + 1])

        def norm_act(act, col, meta=False):
            for t in range(T):
                alink(act, nc.scalar.activation(SQ, x[:, t, :], ACT.Square, accum_out=stat[:, t:t + 1]))
            if meta:
                alink(act, nc.scalar.activation(SQ[0:META], xm[:, :], ACT.Square, accum_out=stat[0:META, 2:3]))
                root_act(act, slice(2, 3), D, 0, META)
            root_act(act, slice(0, T), D, 0)
            act_end(act)
            act_end(act)
            if col is not None:
                for k in range(1, KD, 2):
                    n = act_a()
                    act.wait_ge(to_act, n)
                    lo = 0 if meta else META
                    nc.scalar.activation(hT[:, k, lo:], bank_a(n)[:, 0:L2 - lo], ACT.Copy,
                                         scale=col[:, k:k + 1]).then_inc(act_out, 1)
                act_end(act)

        def rstd_dve(dve, cols, rows=P):
            dlink(dve, nc.vector.reciprocal(stat[0:rows, cols], stat[0:rows, cols]))

        def norm_dve(dve, col, meta=False):
            dve_end(dve)
            rstd_dve(dve, slice(0, T))
            if meta:
                rstd_dve(dve, slice(2, 3), META)
                nc.vector.tensor_scalar(XMN, xm[:, :], stat[0:META, 2:3], None, ALU.mult)
            for t in range(T):
                nc.vector.tensor_scalar(xn[:, t, :], x[:, t, :], stat[:, t:t + 1], None, ALU.mult)
            dve_end(dve)
            if col is not None:
                for k in range(0, KD, 2):
                    n = dve_d()
                    dve.wait_ge(to_dve, n)
                    lo = 0 if meta else META
                    nc.vector.tensor_scalar(hT[:, k, lo:], bank_d(n)[:, 0:L2 - lo], col[:, k:k + 1],
                                            None, ALU.mult).then_inc(dve_out, 1)
                dve_end(dve)

        def norm_pe(pe, meta=False, last=False):
            pe_end(pe)
            pe_end(pe)
            if last:
                return
            for k in range(KD):
                if k % 2 == 0:
                    n, to, bank = pe_d(), to_dve, bank_d
                    if n > 4:
                        pe.wait_ge(dve_out, n - 4)
                else:
                    n, to, bank = pe_a(), to_act, bank_a
                    if n > 4:
                        pe.wait_ge(act_out, n - 4)
                o = bank(n)
                c = 0
                if meta:
                    nc.tensor.transpose(o[:, 0:META], XMN[:, k * P:(k + 1) * P], ident[0:META, 0:META])
                    c = META
                for t in range(T):
                    m = nc.tensor.transpose(o[:, c + t * P:c + (t + 1) * P], xn[:, t, k * P:(k + 1) * P], ident)
                m.then_inc(to, 1)
            pe_end(pe)

        def resid_pe(pe):
            pe_end(pe)
            pe_end(pe)

        def resid_act(act, normed=True):
            if normed:
                for t in range(T):
                    alink(act, nc.scalar.activation(SQ, ps[:, 2 * t:2 * t + 2, :], ACT.Square,
                                                    accum_out=stat[:, t:t + 1]))
                root_act(act, slice(0, T), D, 0)
            act_end(act)
            act_end(act)

        def resid_dve(dve, gain, factor):
            dve_end(dve)
            rstd_dve(dve, slice(0, T))
            if factor != 1.0:
                dlink(dve, nc.vector.tensor_scalar(stat[:, 0:T], stat[:, 0:T], factor, None, ALU.mult))
            for t in range(T):
                dlink(dve, nc.vector.scalar_tensor_tensor(
                    xn[:, t, :], ps[:, 2 * t:2 * t + 2, :].rearrange("p a b -> p (a b)"), stat[:, t:t + 1],
                    gains[:, gain, :], ALU.mult, ALU.mult))
                nc.vector.tensor_tensor(x[:, t, :], x[:, t, :], xn[:, t, :], ALU.add)
            dve_end(dve)

        def product_pe(pe, s0, nk, lhs, meta=False):
            for k in range(nk):
                n = s0 + k // 2
                if k % 2 == 0:
                    take_slot(pe, n)
                for t in range(T):
                    for h in range(2):
                        m = nc.tensor.matmul(ps[:, 2 * t + h, :], lhs(k, t), slot2(n)[:, k % 2, h * 512:(h + 1) * 512],
                                             start=(k == 0), stop=(k == nk - 1))
                if meta:
                    for h in range(2):
                        m = nc.tensor.matmul(ps[0:META, 4 + h, :], lhs(k, T), slot2(n)[:, k % 2, h * 512:(h + 1) * 512],
                                             start=(k == 0), stop=(k == nk - 1))
                if k % 2 == 1:
                    m.then_inc(slot_used, 1)
            pe_end(pe)

        gate_s = arena[:, 4096:4608].rearrange("p (b n) -> p b n", b=2)
        hid = arena[:, 4608:5120].rearrange("p (b n) -> p b n", b=2)
        NF = 2 * NPAIR

        def ffn_pe(pe, call):
            s0 = at[("ffn", call)]
            b0 = NF * call

            def gateup(j, it=None):
                q, c = j // 2, j % 2
                off = 0 if it is None else it * 4
                if c == 0:
                    for w in (3 * q, 3 * q + 1):
                        pe.wait_ge(slot_in[(s0 + w) % NSLOT], slot_value[s0 + w] + (0 if it is None else it * 16))
                if j >= 2 or it is not None:
                    pe.wait_ge(hidden, off + (b0 + j - 1))
                for w in range(2):
                    for k in range(KD):
                        m = nc.tensor.matmul(ps[:, 4 + j % 2, 256 * w:256 * (w + 1)],
                                             slot8(s0 + 3 * q + w)[:, k, c * P:(c + 1) * P], hT[:, k, META:],
                                             start=(k == 0), stop=(k == KD - 1))
                        if c == 1 and w == 0 and k == 0 and (j > 1 or it is not None):
                            m.then_inc(slot_used, 1)
                    if c == 1 and w == 0:
                        m.then_inc(slot_used, 1)
                m.then_inc(gate_up, 1)

            def down_tile(j, it=None):
                q, c = j // 2, j % 2
                off = 0 if it is None else it * 4
                if c == 0:
                    pe.wait_ge(slot_in[(s0 + 3 * q + 2) % NSLOT],
                               slot_value[s0 + 3 * q + 2] + (0 if it is None else it * 16))
                pe.wait_ge(hidden, off + (b0 + j + 1))
                for t in range(T):
                    for h in range(2):
                        m = nc.tensor.matmul(ps[:, 2 * t + h, :], hid[:, j % 2, t * P:(t + 1) * P],
                                             slot2(s0 + 3 * q + 2)[:, c, h * 512:(h + 1) * 512],
                                             start=(j == 0 and it is None), stop=(j == NF - 1))
                        if c == 0 and t == 0 and h == 0:
                            m.then_inc(slot_used, 1)
                m.then_inc(down, 1)

            gateup(0)
            for j in range(4):
                gateup(j + 1)
                down_tile(j)
            with pe.Fori(1, NPAIR // 2) as i:
                for j in range(4):
                    gateup(j + 1, i)
                    down_tile(j, i)
            for j in range(4 * (NPAIR // 2), NF):
                if j + 1 < NF:
                    gateup(j + 1)
                down_tile(j)
            pe.drain().then_inc(slot_used, 1)
            pe_end(pe)

        def ffn_act(act, call):
            b0 = NF * call

            def tile(j, off=0):
                act.wait_ge(gate_up, off + (b0 + j + 1))
                if b0 + j >= 2 or not isinstance(off, int):
                    act.wait_ge(hidden, off + (b0 + j - 1))
                nc.scalar.activation(gate_s[:, j % 2, :], ps[:, 4 + j % 2, 0:256], ACT.Silu).then_inc(silu_done, 1)

            tile(0)
            tile(1)
            with act.Fori(1, NPAIR) as i:
                tile(0, i * 2)
                tile(1, i * 2)
            act_end(act)

        def ffn_dve(dve, call):
            b0 = NF * call

            def tile(j, off=0):
                dve.wait_ge(silu_done, off + (b0 + j + 1))
                if b0 + j >= 2 or not isinstance(off, int):
                    dve.wait_ge(down, off + (b0 + j - 1))
                nc.vector.tensor_tensor(hid[:, j % 2, :], gate_s[:, j % 2, :], ps[:, 4 + j % 2, 256:512],
                                        ALU.mult).then_inc(hidden, 1)

            tile(0)
            tile(1)
            with dve.Fori(1, NPAIR) as i:
                tile(0, i * 2)
                tile(1, i * 2)
            dve_end(dve)

        rowsA, rowsB = arena[0:NROW_A, 0:P], arena[0:NROW_B, P:2 * P]
        pe_rows = arena[0:64, 2 * P:2 * P + 64]

        def rows(v):
            return v.rearrange("(r n) -> r n", n=P)

        def everywhere(v):
            return v.rearrange("(o n) -> o n", o=1).broadcast_to([P, v.shape[0]])

        def first_loads(eng):
            def load(dst, src):
                eng.dma_start(dst, src).then_inc(first_in, 16)
                n_first()

            for t in range(T):
                load(x[:, t, :], d["x"][0, t * P:(t + 1) * P, :])
            load(cst[:, :], d["consts"])
            for i, (l, g) in enumerate((l, g) for l in range(2) for g in (0, 2, 4)):
                load(rowsA[8 * i:8 * i + 8, :], rows(d["norm_gains"][l, g]))
            load(rowsA[48:96, :], d["b_conv_w"][0].rearrange("c o (r n) -> (c o r) n", n=P))
            load(rowsA[96:108, :], rows(d["b_conv_b"][0]))
            load(rowsA[108:116, :], rows(d["b_norm_w"][0]))
            load(rowsB[0:48, :], d["c_mu"][0].rearrange("c (r n) -> (c r) n", n=P))
            for i, n in enumerate(("c_w0", "c_a0", "c_k_k", "c_k_a")):
                load(rowsB[48 + 8 * i:56 + 8 * i, :], rows(d[n][0]))
            load(rowsB[80:88, :], d["c_r_k"][0].rearrange("(r a) n -> r (a n)", a=2))
            load(rowsB[88:104, :], d["norm_g_2"].rearrange("l (r n) -> (l r) n", n=P))
            load(pe_rows[0:32, :], d["a_cmp_pe_k"][0])
            load(pe_rows[32:64, :], d["a_cmp_pe_v"][0])

        def later_loads(eng):
            def load(dst, src):
                eng.dma_start(dst, src).then_inc(later_in, 16)
                n_later()

            for i, (l, g) in enumerate((l, g) for l in range(2) for g in (1, 3, 5)):
                load(gains[:, i, :], everywhere(d["norm_gains"][l, g]))
            load(gains[:, LN_G, :], everywhere(d["c_ln_g"][0]))
            load(gains[:, LN_B, :], everywhere(d["c_ln_b"][0]))
            for l in range(2):
                load(gains[:, SUBLN, l * 512:(l + 1) * 512], everywhere(d["subln_g_2"][l]))
            load(gains[:, FINAL_G, :], everywhere(d["final_g_2"]))
            for l in range(2):
                for i, n in enumerate(("lam_q1_2", "lam_k1_2", "lam_q2_2", "lam_k2_2")):
                    c = (4 * l + i) * 64
                    load(gains[:, LAMB, c:c + 64], everywhere(d[n][l]))
            load(dt_bias, everywhere(d["b_dt_bias"][0]))
            load(a_log, everywhere(d["b_a_log"][0]))
            load(d_skip, everywhere(d["b_d_skip"][0]))
            for l in range(2):
                load(forget[:, l:l + 1], d["b_forget_2"][l].rearrange("(p o) -> p o", o=1))
            load(w2k[:, 0:64], d["a_cmp_w2_k"][0])
            load(w2k[:, 64:128], d["a_cmp_w2_k"][0])
            load(w2v, d["a_cmp_w2_v"][0])
            load(xm[:, :], d["meta_tokens_2"])

        def prep_pe(pe):
            pe.wait_ge(first_in, 16 * n_first.n)
            nc.tensor.transpose(ps[:, 0, 0:NROW_A], rowsA, ident[0:NROW_A, 0:NROW_A])
            nc.tensor.transpose(ps[:, 0, P:P + NROW_B], rowsB, ident[0:NROW_B, 0:NROW_B])
            nc.tensor.transpose(ps[0:64, 0, 256:320], pe_rows, ident[0:64, 0:64])
            pe_end(pe)
            pe_end(pe)

        def prep_act(act):
            act.wait_ge(first_in, 16 * n_first.n)
            act_end(act)
            act_end(act)

        def prep_dve(dve):
            dve.wait_ge(first_in, 16 * n_first.n)
            dve_end(dve)
            nc.vector.tensor_copy(colA[:, :], ps[:, 0, 0:NROW_A])
            nc.vector.tensor_copy(colB[:, :], ps[:, 0, P:P + NROW_B])
            nc.vector.tensor_copy(small[0:64, 128:192], ps[0:64, 0, 256:320])
            dve_end(dve)

        sc_ready, sc_masked, exp_done, p_ready = sem("sc_ready"), sem("sc_masked"), sem("exp_done"), sem("p_ready")
        pt_ready, pt_copied, o_ready, o_taken = sem("pt_ready"), sem("pt_copied"), sem("o_ready"), sem("o_taken")
        pe_u, act_u, dve_u = Turn(), Turn(), Turn()
        SCW = 2 * L2
        NB = 3
        att = arena[:, 14200:14200 + 2 * NB * SCW + 2 * 512 + 8 * NB]
        prob = att[:, 0:NB * SCW].rearrange("p (b c n) -> p b c n", b=NB, c=2)
        scor = att[:, NB * SCW:2 * NB * SCW].rearrange("p (b c n) -> p b c n", b=NB, c=2)
        probT = att[:, 2 * NB * SCW:2 * NB * SCW + 1024].rearrange("p (b n) -> p b n", b=2)
        astat = att[:, 2 * NB * SCW + 1024:2 * NB * SCW + 1024 + 8 * NB].rearrange("p (b n) -> p b n", b=NB)

        def attend_pe(pe, units, scores, blocks, values):
            n0 = pe_u.n
            for i in range(len(units) + 3):
                if i < len(units):
                    u, n = units[i], pe_u()
                    if n > 2:
                        pe.wait_ge(sc_masked, n - 2)
                    for c in range(2):
                        for o, pairs in scores(u, c, ps[:, 2 * (n % 2) + c, :]):
                            m = group(o, pairs)
                    m.then_inc(sc_ready, 1)
                if 2 <= i <= len(units) + 1:
                    u, n = units[i - 2], n0 + i - 1
                    pe.wait_ge(p_ready, n)
                    if n > 2:
                        pe.wait_ge(pt_copied, n - 2)
                    for src, rows, keys, col in blocks(u, n % NB):
                        m = nc.tensor.transpose(ps[0:keys, 4 + n % 2, col:col + rows], src, ident[0:rows, 0:rows])
                    m.then_inc(pt_ready, 1)
                if i >= 3:
                    u, n = units[i - 3], n0 + i - 2
                    pe.wait_ge(pt_copied, n)
                    if n > 2:
                        pe.wait_ge(o_taken, n - 2)
                    m = group(*values(u, n % 2, ps[:, 6 + n % 2, :]))
                    m.then_inc(o_ready, 1)
            pe_end(pe)

        def attend_act(act, units, rows, width, ptcols, comps=lambda u: 2):
            n0 = act_u.n
            for i in range(len(units) + 2):
                if i < len(units):
                    u, n = units[i], act_u()
                    act.wait_ge(sc_masked, n)
                    r, w, b = rows(u), width(u), n % NB
                    for c in range(comps(u)):
                        m = nc.scalar.activation(prob[0:r, b, c, 0:w], scor[0:r, b, c, 0:w], ACT.Exp,
                                                 bias=astat[0:r, b, c:c + 1], accum_out=astat[0:r, b, 2 + c:3 + c])
                    m.then_inc(exp_done, 1)
                if i >= 2:
                    u, n = units[i - 2], n0 + i - 1
                    act.wait_ge(pt_ready, n)
                    if n > 2:
                        act.wait_ge(o_ready, n - 2)
                    for keys, c0, c1 in ptcols(u):
                        m = nc.scalar.activation(probT[0:keys, n % 2, c0:c1], ps[0:keys, 4 + n % 2, c0:c1], ACT.Copy)
                    m.then_inc(pt_copied, 1)
            act_end(act)

        def attend_dve(dve, units, rows, width, mask, combine, take, comps=lambda u: 2):
            n0 = dve_u.n
            for i in range(len(units) + 3):
                if i < len(units):
                    u, n = units[i], dve_u()
                    r, w, ncomp, b = rows(u), width(u), comps(u), n % NB
                    dve.wait_ge(sc_ready, n)
                    if n > NB:
                        dve.wait_ge(exp_done, n - NB)
                    for c in range(ncomp):
                        m = nc.vector.tensor_tensor(scor[0:r, b, c, 0:w], ps[0:r, 2 * (n % 2) + c, 0:w], mask(u), ALU.add)
                    dlink(dve, m)
                    nc.vector.tensor_reduce(astat[0:r, b, 0:ncomp], scor[0:r, b, 0:ncomp, 0:w], AX, ALU.max,
                                            negate=True).then_inc(sc_masked, 1)
                if 1 <= i <= len(units):
                    u, n = units[i - 1], n0 + i
                    dve.wait_ge(exp_done, n)
                    r, ncomp, b = rows(u), comps(u), n % NB
                    dlink(dve, nc.vector.reciprocal(astat[0:r, b, 4:4 + ncomp], astat[0:r, b, 2:2 + ncomp]))
                    combine(dve, u, b).then_inc(p_ready, 1)
                if i >= 3:
                    u, n = units[i - 3], n0 + i - 2
                    dve.wait_ge(o_ready, n)
                    take(dve, u, n % 2, ps[:, 6 + n % 2, :]).then_inc(o_taken, 1)
            dve_end(dve)

        fm = arena[:, 0:1536].rearrange("p (j n) -> p j n", j=6)
        kv = arena[0:64, 1536:2560].rearrange("p (w h n) -> p w h n", w=2, h=2)
        vtok = arena[:, 2560:3072].rearrange("p (t w n) -> p t w n", t=T, w=2)
        gsm = arena[:, 3072:3328]
        glog = gsm[:, 0:80].rearrange("p (t n) -> p t n", t=T)
        gates = gsm[:, 80:128].rearrange("p (t h c) -> p t h c", t=T, c=3)
        zs = arena[:, 3328:5376].rearrange("p (t n) -> p t n", t=T)
        oa = arena[:, 5376:6400].rearrange("p (t n) -> p t n", t=T)
        XP = 3 + S
        xpad = arena[:, 6400:6400 + 12 * XP].rearrange("p (i n) -> p i n", i=12)
        xc = arena[:, 9600:12672].rearrange("p (i n) -> p i n", i=12)
        rtmp = arena[:, 12672:13696].rearrange("p (b n) -> p b n", b=2)
        kcmp, vcmp = arena[:, 13696:13726], arena[0:NCMP, 13728:13856].rearrange("p (g n) -> p g n", g=2)
        hidk = arena[0:64, 13856:13916].rearrange("p (w n) -> p w n", w=2)
        blk = arena[0:64, 14200:16120].rearrange("p (w l h n) -> p w l h n", w=2, l=32, h=2)
        ctmp = arena[:, 16120:16120 + 256]
        pcmp = arena[:, 17500:17740].rearrange("p (t h n) -> p t h n", t=T, h=NH)
        pstat = arena[:, 17740:17760]

        NS = range(12)

        def mixer_pe(pe):
            s = at["mixer"]
            hk = lambda k: hT[:, k, META:]

            def wait_d(n):
                if n > 4:
                    pe.wait_ge(dve_out, n - 4)

            def wait_a(n):
                if n > 4:
                    pe.wait_ge(act_out, n - 4)

            def fm_tile(w, c0, rows=P, o=None, n=None):
                return group(o, [(w[:, k, c0:c0 + rows], hk(k)) for k in range(KD)])

            for j in range(4):
                if j % 2 == 0:
                    take_slot(pe, s)
                n = pe_d()
                wait_d(n)
                fm_tile(slot8(s), (j % 2) * P, o=bank_d(n)[:, 0:S]).then_inc(to_dve, 1)
                if j % 2 == 1:
                    pe.drain().then_inc(slot_used, 1)
                    s += 1
            take_slot(pe, s)
            for w in range(2):
                n = pe_d()
                wait_d(n)
                for h in range(2):
                    m = fm_tile(slot8(s), w * P + h * 64, 64, bank_d(n)[0:64, h * S:(h + 1) * S])
                m.then_inc(to_dve, 1)
            pe.drain().then_inc(slot_used, 1)
            s += 1
            for w in range(2):
                take_slot(pe, s)
                n = pe_d()
                wait_d(n)
                fm_tile(slot8(s), 0, o=bank_d(n)[:, 0:S]).then_inc(to_dve, 1)
                n = pe_d()
                wait_d(n)
                for t in range(T):
                    m = group(bank_d(n)[:, t * P:(t + 1) * P],
                              [(hT[:, k, META + t * P:META + (t + 1) * P], slot8(s)[:, k, P:2 * P]) for k in range(KD)])
                m.then_inc(to_dve, 1)
                pe.drain().then_inc(slot_used, 1)
                s += 1
            take_slot(pe, s)
            n = pe_d()
            wait_d(n)
            for t in range(T):
                m = group(bank_d(n)[:, t * 40:(t + 1) * 40],
                          [(hT[:, k, META + t * P:META + (t + 1) * P], slot8(s)[:, k, 0:40]) for k in range(KD)])
            m.then_inc(to_dve, 1)
            pe.drain().then_inc(slot_used, 1)
            s += 1
            for c in range(4):
                take_slot(pe, s)
                n = pe_a()
                wait_a(n)
                for t in range(T):
                    m = group(bank_a(n)[:, t * 256:(t + 1) * 256],
                              [(hT[:, k, META + t * P:META + (t + 1) * P], slot8(s)[:, k, :]) for k in range(KD)])
                m.then_inc(to_act, 1)
                pe.drain().then_inc(slot_used, 1)
                s += 1
            for i in range(12):
                if i % 2 == 0:
                    take_slot(pe, s)
                n = pe_d()
                wait_d(n)
                fm_tile(slot8(s), (i % 2) * P, o=bank_d(n)[:, 0:S]).then_inc(to_dve, 1)
                if i % 2 == 1:
                    pe.drain().then_inc(slot_used, 1)
                    s += 1
            pe_end(pe)
            for j in range(6):
                n = pe_d()
                wait_d(n)
                group(bank_d(n)[:, 0:S], [(const("rot"), fm[:, j, :])]).then_inc(to_dve, 1)
            n = pe_d()
            wait_d(n)
            group(bank_d(n)[0:64, :], [(const("rot", 64)[:, 0:64], kv[:, 0, :, :])]).then_inc(to_dve, 1)
            pe_end(pe)
            for w in range(2):
                take_slot(pe, s)
                n = pe_a()
                wait_a(n)
                w1 = ring[0:64, s % NSLOT, :].rearrange("p (l e) -> p l e", l=32)
                group(bank_a(n)[0:64, 0:30], [(w1[:, l, :], blk[:, w, l, :, :]) for l in range(32)]).then_inc(to_act, 1)
                pe.drain().then_inc(slot_used, 1)
                s += 1
            pe_end(pe)
            n = pe_d()
            wait_d(n)
            group(bank_d(n)[:, 0:30], [(w2k, hidk[:, 0, :])])
            for g in range(2):
                m = group(bank_d(n)[0:NCMP, 32 + g * 64:96 + g * 64],
                          [(hidk[:, 1, g * NCMP:(g + 1) * NCMP], w2v)])
            m.then_inc(to_dve, 1)
            pe_end(pe)
            for t in range(T):
                for g in range(NKV):
                    n = pe_d()
                    wait_d(n)
                    for j in range(4):
                        m = group(bank_d(n)[:, j * NCMP:(j + 1) * NCMP],
                                  [(fm[g * 64:g * 64 + 64, j, t * P:(t + 1) * P],
                                    kcmp[g * 64:g * 64 + 64, g * NCMP:(g + 1) * NCMP])])
                    m.then_inc(to_dve, 1)
            pe_end(pe)

            def scores(u, c, bank):
                t, h = u
                g, j, w = h // 4, h % 4, (t + 1) * P
                return [(bank[:, 0:w], [(fm[g * 64:g * 64 + 64, j, t * P:(t + 1) * P], fm[g * 64:g * 64 + 64, 4 + c, 0:w])])]

            def blocks(u, b):
                t, h = u
                out = [(prob[:, b, c, k * P:(k + 1) * P], P, P, (c * (t + 1) + k) * P) for c in range(2) for k in range(t + 1)]
                return out

            def values(u, b, bank):
                t, h = u
                g = h // 4
                pairs = [(pcT[:, t, h, :], vcmp[:, g, :])]
                for c in range(2):
                    for k in range(t + 1):
                        col = (c * (t + 1) + k) * P
                        pairs.append((probT[:, b, col:col + P], vtok[:, k, c, g * 64:(g + 1) * 64]))
                return bank[:, 0:64], pairs

            pe_end(pe)
            pe_end(pe)
            for t in range(T):
                for h4 in range(2):
                    n = pe_a()
                    wait_a(n)
                    for h in range(4):
                        m = nc.tensor.transpose(bank_a(n)[0:NCMP, h * P:(h + 1) * P], pcmp[:, t, h4 * 4 + h, :], ident)
                    m.then_inc(to_act, 1)
            pe_end(pe)
            attend_pe(pe, ATT_UNITS, scores, blocks, values)
            ssd_pe(pe, wait_d, wait_a)
            product_pe(pe, at["mixer_out"], 12, lambda k, t: mT[:, k, t * P:(t + 1) * P])

        pcT = arena[0:NCMP, 6400:6400 + 2048].rearrange("p (t h n) -> p t h n", t=T, h=NH)
        ATT_UNITS = [(t, h) for t in range(T) for h in range(NH)]

        def mixer_act(act):
            for c in range(4):
                n = act_a()
                act.wait_ge(to_act, n)
                m = nc.scalar.activation(zs[:, :, c * 256:(c + 1) * 256],
                                         bank_a(n).rearrange("p (t n) -> p t n", t=T), ACT.Silu)
                m.then_inc(act_out, 1)
            act_end(act)
            for i in range(12):
                nc.scalar.activation(xc[:, i, :], xc[:, i, :], ACT.Silu, bias=colA[:, 96 + i:97 + i])
            nc.scalar.activation(gates[:, :, :, :].rearrange("p t h c -> p t (h c)"), glog[:, :, 0:24], ACT.Sigmoid)
            act_end(act)
            for w in range(2):
                n = act_a()
                act.wait_ge(to_act, n)
                nc.scalar.activation(hidk[:, w, :], bank_a(n)[0:64, 0:30], ACT.Silu).then_inc(act_out, 1)
            act_end(act)
            act_end(act)
            act_end(act)
            nc.scalar.activation(pcmp[:, :, :, :], pcmp[:, :, :, :], ACT.Exp)
            act_end(act)
            act_end(act)
            for t in range(T):
                for h4 in range(2):
                    n = act_a()
                    act.wait_ge(to_act, n)
                    nc.scalar.activation(pcT[:, t, h4 * 4:h4 * 4 + 4, :],
                                         bank_a(n)[0:NCMP, :].rearrange("p (h n) -> p h n", h=4), ACT.Copy).then_inc(act_out, 1)
            act_end(act)
            attend_act(act, ATT_UNITS, lambda u: P, lambda u: (u[0] + 1) * P, lambda u: [(P, 0, 256 * (u[0] + 1))])
            ssd_act(act)
            act_end(act)

        def rope_dve(dve, j, raw, rotated, cos, sin, scale):
            tmp = rtmp[0:raw.shape[0], j % 2, :]
            tmp = tmp[:, 0:256 * (1 if len(raw.shape) == 2 else raw.shape[1])]
            if len(raw.shape) == 3:
                tmp = tmp.rearrange("p (h n) -> p h n", h=raw.shape[1])
            m = nc.vector.tensor_tensor(tmp, rotated, sin, ALU.mult)
            m.then_inc(dve_out, 1)
            dlink(dve, nc.vector.tensor_tensor(raw, raw, cos, ALU.mult))
            if scale == 1.0:
                return nc.vector.tensor_tensor(raw, raw, tmp, ALU.add)
            dlink(dve, nc.vector.tensor_tensor(raw, raw, tmp, ALU.add))
            return nc.vector.tensor_scalar(raw, raw, scale, None, ALU.mult)

        def mixer_dve(dve):
            def taken(dst, src):
                nc.vector.tensor_copy(dst, src).then_inc(dve_out, 1)

            def next_d():
                n = dve_d()
                dve.wait_ge(to_dve, n)
                return bank_d(n)

            nc.vector.memset(xpad[:, :, 0:3], 0.0)
            for j in range(4):
                taken(fm[:, j, :], next_d()[:, 0:S])
            for w in range(2):
                taken(kv[:, w, :, :], next_d()[0:64, :].rearrange("p (h n) -> p h n", h=2))
            for w in range(2):
                taken(fm[:, 4 + w, :], next_d()[:, 0:S])
                taken(vtok[:, :, w, :], next_d()[:, 0:S].rearrange("p (t n) -> p t n", t=T))
            taken(glog[:, :, :], next_d()[:, 0:80].rearrange("p (t n) -> p t n", t=T))
            for i in range(12):
                b = next_d()
                ins = nc.vector.tensor_copy(xpad[:, i, 3:XP], b[:, 0:S])
                ins.then_inc(dve_out, 1)
                dve.wait_ge(dve_out, dve_d.n)
                cw = lambda c: colA[:, 48 + 12 * c + i:49 + 12 * c + i]
                dlink(dve, nc.vector.tensor_scalar(xc[:, i, :], xpad[:, i, 0:S], cw(0), None, ALU.mult))
                for c in range(1, 4):
                    dlink(dve, nc.vector.scalar_tensor_tensor(xc[:, i, :], xpad[:, i, c:c + S], cw(c), xc[:, i, :],
                                                              ALU.mult, ALU.add))
            dve_end(dve)
            cos, sin = const("cos"), const("sin")
            for j in range(6):
                rope_dve(dve, j, fm[:, j, :], next_d()[:, 0:S], cos[:, 0:S], sin[:, 0:S], SCR if j < 4 else 1.0)
            bc = lambda a: a[0:64, 0:S].rearrange("p (o n) -> p o n", o=1).broadcast_to([64, 2, S])
            dlink(dve, rope_dve(dve, 0, kv[:, 0, :, :], next_d()[0:64, :].rearrange("p (h n) -> p h n", h=2),
                                bc(cos), bc(sin), 1.0))
            for w in range(2):
                for h in range(2):
                    view = kv[:, w, h, :].rearrange("p (n s) -> p s n", s=16)
                    for a in range(2):
                        pos = peT[w][:, a * 16:(a + 1) * 16].rearrange("p (s o) -> p s o", o=1).broadcast_to([64, 16, NCMP])
                        nc.vector.tensor_tensor(blk[:, w, a * 16:(a + 1) * 16, h, :], view[:, :, a:a + NCMP], pos, ALU.add)
            dve_end(dve)
            dve_end(dve)
            b = next_d()
            nc.vector.tensor_copy(kcmp, b[:, 0:30])
            taken(vcmp[:, :, :], b[0:NCMP, 32:160].rearrange("p (g n) -> p g n", g=2))
            dve_end(dve)
            for t in range(T):
                madd = const("cmpadd")[:, t * NCMP:(t + 1) * NCMP].rearrange("p (o n) -> p o n", o=1).broadcast_to([P, 4, NCMP])
                for g in range(NKV):
                    nc.vector.tensor_tensor(pcmp[:, t, 4 * g:4 * g + 4, :],
                                            next_d()[:, 0:4 * NCMP].rearrange("p (h n) -> p h n", h=4),
                                            madd, ALU.add).then_inc(dve_out, 1)
                dve.wait_ge(dve_out, dve_d.n)
                mx = stat[:, 16:24]
                dlink(dve, nc.vector.tensor_reduce(mx, pcmp[:, t, :, :], AX, ALU.max))
                dlink(dve, nc.vector.tensor_tensor(pcmp[:, t, :, :], pcmp[:, t, :, :],
                                                   mx.rearrange("p (h o) -> p h o", o=1).broadcast_to([P, NH, NCMP]), ALU.subtract))
            dve_end(dve)
            dve_end(dve)
            for t in range(T):
                mmul = const("cmpmul")[:, t * NCMP:(t + 1) * NCMP].rearrange("p (o n) -> p o n", o=1).broadcast_to([P, NH, NCMP])
                sm = stat[:, 16:24]
                bsm = sm.rearrange("p (h o) -> p h o", o=1)
                dlink(dve, nc.vector.tensor_tensor(pcmp[:, t, :, :], pcmp[:, t, :, :], mmul, ALU.mult))
                dlink(dve, nc.vector.tensor_reduce(sm, pcmp[:, t, :, :], AX, ALU.add))
                dlink(dve, nc.vector.tensor_scalar(sm, sm, 1e-30, None, ALU.max))
                dlink(dve, nc.vector.reciprocal(sm, sm))
                dlink(dve, nc.vector.tensor_tensor(bsm, bsm, gates[:, t, :, 0:1], ALU.mult))
                dlink(dve, nc.vector.tensor_tensor(pcmp[:, t, :, :], pcmp[:, t, :, :], bsm.broadcast_to([P, NH, NCMP]), ALU.mult))
            dve_end(dve)
            dve_end(dve)

            def combine(dve, u, b):
                t, h = u
                dlink(dve, nc.vector.tensor_tensor(astat[:, b, 4:6], astat[:, b, 4:6], gates[:, t, h, 1:3], ALU.mult))
                w = (t + 1) * P
                return nc.vector.tensor_tensor(prob[:, b, :, 0:w], prob[:, b, :, 0:w],
                                               astat[:, b, 4:6].rearrange("p (c o) -> p c o", o=1).broadcast_to([P, 2, w]), ALU.mult)

            def take(dve, u, b, bank):
                t, h = u
                return nc.vector.tensor_copy(oa[:, t, h * 64:(h + 1) * 64], bank[:, 0:64])

            attend_dve(dve, ATT_UNITS, lambda u: P, lambda u: (u[0] + 1) * P,
                       lambda u: qmask[:, L2 - (u[0] + 1) * P:], combine, take)
            ssd_dve(dve, next_d)
            dve_end(dve)

        ea = arena[:, 0:512]
        dtv = ea[:, 0:32].rearrange("p (t h) -> p t h", t=T)
        dA = ea[:, 32:64].rearrange("p (t h) -> p t h", t=T)
        acs = ea[:, 64:96].rearrange("p (t h) -> p t h", t=T)
        eacs = ea[:, 96:112]
        dec = ea[:, 112:128]
        nega = ea[:, 128:144]
        sp_a, sp_b = ea[:, 144:176].rearrange("p (t h) -> p t h", t=T), ea[:, 176:208].rearrange("p (t h) -> p t h", t=T)
        acsT = ea[0:16, 208:464].rearrange("p (t n) -> p t n", t=T)
        cb = arena[:, 512:1024].rearrange("p (i n) -> p i n", i=4)
        seg = arena[:, 1024:3072].rearrange("p (b h n) -> p b h n", b=4, h=4)
        xst = arena[:, 6400:8448].rearrange("p (t n) -> p t n", t=T)
        xdd = arena[:, 8448:9472]
        st = arena[:, 12672:13696].rearrange("p (g n) -> p g n", g=2)
        ys = arena[:, 13700:15748].rearrange("p (t n) -> p t n", t=T)
        xd = arena[:, 15748:17796].rearrange("p (t n) -> p t n", t=T)
        btok = arena[:, 17796:18052].rearrange("p (g n) -> p g n", g=2)
        mT = arena[:, 9600:12672].rearrange("p (i n) -> p i n", i=12)
        seg_exp, seg_out = sem("seg_exp"), sem("seg_out")
        seg_base, seg_first = [], []
        UQ = [(t, q) for t in range(T) for q in range(4)]

        def byhead(a, rows=P):
            return a.rearrange("p (h n) -> p h n", n=64)

        def perhead(a):
            return a.rearrange("p (h o) -> p h o", o=1).broadcast_to([a.shape[0], a.shape[1], 64])

        def ssd_pe(pe, wait_d, wait_a):
            for t in range(T):
                for q in range(2):
                    n = pe_a()
                    wait_a(n)
                    for i in range(4):
                        m = nc.tensor.transpose(bank_a(n)[:, i * P:(i + 1) * P], xc[:, 4 * q + i, t * P:(t + 1) * P], ident)
                    m.then_inc(to_act, 1)
            n = pe_a()
            wait_a(n)
            for g in range(2):
                m = nc.tensor.transpose(bank_a(n)[:, g * P:(g + 1) * P], xc[:, 8 + g, 0:P], ident)
            m.then_inc(to_act, 1)
            n = pe_a()
            wait_a(n)
            for t in range(T):
                for g in range(2):
                    i = 2 * t + g
                    m = group(bank_a(n)[:, i * P:(i + 1) * P],
                              [(xc[:, 8 + g, t * P:(t + 1) * P], xc[:, 10 + g, t * P:(t + 1) * P])])
            m.then_inc(to_act, 1)
            pe_end(pe)
            pe_end(pe)
            pe_end(pe)
            n = pe_d()
            wait_d(n)
            b = bank_d(n)
            for t in range(T):
                group(b[:, t * 16:(t + 1) * 16], [(const("upper"), dA[:, t, :])])
                group(b[0:16, 64 + t * P:64 + (t + 1) * P], [(dA[:, t, :], const("upper"))])
            group(b[:, 32:48], [(ones, dA[:, 0, :])]).then_inc(to_dve, 1)
            pe_end(pe)
            pe_end(pe)
            pe_end(pe)
            seg_base.append(pe_a.n)
            seg_first.append(pe_d.n)
            for i in range(len(UQ) + 1):
                if i < len(UQ):
                    t, q = UQ[i]
                    n = pe_d()
                    wait_d(n)
                    for h in range(4):
                        hh = 4 * q + h
                        m = group(bank_d(n)[:, h * P:(h + 1) * P],
                                  [(ident[0:16, hh:hh + 1].broadcast_to([16, P]), acsT[:, t, :])])
                    m.then_inc(to_dve, 1)
                if i >= 1:
                    t, q = UQ[i - 1]
                    pe.wait_ge(seg_out, i)
                    n = pe_a()
                    wait_a(n)
                    for h in range(4):
                        hh = 4 * q + h
                        m = group(bank_a(n)[:, h * 64:(h + 1) * 64], [(seg[:, (i - 1) % 4, h, :], xd[:, t, hh * 64:(hh + 1) * 64])])
                    m.then_inc(to_act, 1)
            for g in range(2):
                n = pe_a()
                wait_a(n)
                group(bank_a(n), [(btok[:, g, :], xdd[:, g * 512:(g + 1) * 512])]).then_inc(to_act, 1)
            pe_end(pe)
            for g in range(2):
                n = pe_d()
                wait_d(n)
                group(bank_d(n), [(xc[:, 10 + g, P:S], st[:, g, :])]).then_inc(to_dve, 1)
            pe_end(pe)
            pe_end(pe)
            pe_end(pe)
            for k in range(12):
                n = pe_d()
                wait_d(n)
                for t in range(T):
                    src = oa[:, t, k * P:(k + 1) * P] if k < 4 else ys[:, t, (k - 4) * P:(k - 3) * P]
                    m = nc.tensor.transpose(bank_d(n)[:, t * P:(t + 1) * P], src, ident)
                m.then_inc(to_dve, 1)
            pe_end(pe)

        def ssd_act(act):
            def taken(dst, src):
                nc.scalar.activation(dst, src, ACT.Copy).then_inc(act_out, 1)

            def next_a():
                n = act_a()
                act.wait_ge(to_act, n)
                return bank_a(n)

            for t in range(T):
                for q in range(2):
                    taken(xst[:, t, q * 512:(q + 1) * 512], next_a())
            taken(btok[:, :, :], next_a()[:, 0:256].rearrange("p (g n) -> p g n", g=2))
            taken(cb[:, :, :], next_a().rearrange("p (i n) -> p i n", i=4))
            act_end(act)
            alink(act, nc.scalar.activation(sp_b, sp_a, ACT.Abs))
            alink(act, nc.scalar.activation(sp_b, sp_b, ACT.Exp, scale=-1.0))
            nc.scalar.activation(sp_b, sp_b, ACT.Ln, bias=1.0)
            nc.scalar.activation(nega, a_log, ACT.Exp)
            act_end(act)
            act_end(act)
            act_end(act)
            nc.scalar.activation(eacs, acs[:, 1, :], ACT.Exp)
            nc.scalar.activation(dec, dec, ACT.Exp)
            act_end(act)
            act_end(act)
            for i in range(len(UQ) + 1):
                if i < len(UQ):
                    act.wait_ge(dve_out, seg_first[0] + i + 1)
                    nc.scalar.activation(seg[:, i % 4, :, :], seg[:, i % 4, :, :], ACT.Exp).then_inc(seg_exp, 1)
                if i >= 1:
                    t, q = UQ[i - 1]
                    taken(ys[:, t, q * 256:(q + 1) * 256], next_a()[:, 0:256])
            for g in range(2):
                taken(st[:, g, :], next_a())
            act_end(act)
            act_end(act)
            for t in range(T):
                for g in range(2):
                    i = 4 + 2 * t + g
                    alink(act, nc.scalar.activation(xd[:, t, g * 512:(g + 1) * 512], ys[:, t, g * 512:(g + 1) * 512],
                                                    ACT.Square, accum_out=stat[:, i:i + 1]))
            root_act(act, slice(4, 8), 512, 1)
            act_end(act)
            act_end(act)
            act_end(act)

        def ssd_dve(dve, next_d):
            for t in range(T):
                nc.vector.tensor_tensor(sp_a[:, t, :], glog[:, t, 24:40], dt_bias, ALU.add)
            dve_end(dve)
            dve_end(dve)
            dlink(dve, nc.vector.scalar_tensor_tensor(dtv[:, :, :], sp_a[:, :, :], 0.0, sp_b[:, :, :], ALU.max, ALU.add))
            for t in range(T):
                nc.vector.scalar_tensor_tensor(dA[:, t, :], dtv[:, t, :], -1.0, nega, ALU.mult, ALU.mult)
                nc.vector.tensor_tensor(byhead(xd[:, t, :]), byhead(xst[:, t, :]), perhead(dtv[:, t, :]), ALU.mult)
            dve_end(dve)
            b = next_d()
            nc.vector.tensor_copy(acs[:, :, :], b[:, 0:32].rearrange("p (t h) -> p t h", t=T))
            nc.vector.tensor_copy(dec, b[:, 32:48])
            ins = nc.vector.tensor_copy(acsT[:, :, :], b[0:16, 64:320].rearrange("p (t n) -> p t n", t=T))
            ins.then_inc(dve_out, 1)
            dve.wait_ge(dve_out, dve_d.n)
            nc.vector.tensor_tensor(dec, dec, acs[:, 0, :], ALU.subtract)
            dve_end(dve)
            dve_end(dve)
            nc.vector.tensor_tensor(byhead(xdd), byhead(xd[:, 0, :]), perhead(dec), ALU.mult)
            dve_end(dve)
            for i in range(len(UQ) + 1):
                if i < len(UQ):
                    t, q = UQ[i]
                    b = next_d()
                    if i >= 4:
                        dve.wait_ge(to_act, seg_base[0] + i - 3)
                    for h in range(4):
                        hh = 4 * q + h
                        m = nc.vector.scalar_tensor_tensor(seg[:, i % 4, h, :], b[:, h * P:(h + 1) * P], acs[:, t, hh:hh + 1],
                                                           const("segmask"), ALU.subtract, ALU.add)
                    m.then_inc(dve_out, 1)
                if i >= 1:
                    t, q = UQ[i - 1]
                    dve.wait_ge(seg_exp, i)
                    m = nc.vector.tensor_tensor(seg[:, (i - 1) % 4, :, :], seg[:, (i - 1) % 4, :, :],
                                                cb[:, 2 * t + q // 2, :].rearrange("p (o n) -> p o n", o=1).broadcast_to([P, 4, P]),
                                                ALU.mult)
                    m.then_inc(seg_out, 1)
            dve_end(dve)
            for g in range(2):
                b = next_d()
                tmp = xdd[:, g * 512:(g + 1) * 512]
                ins = nc.vector.tensor_tensor(byhead(tmp), byhead(b), perhead(eacs[:, g * 8:(g + 1) * 8]), ALU.mult)
                ins.then_inc(dve_out, 1)
                dve.wait_ge(dve_out, dve_d.n)
                nc.vector.tensor_tensor(ys[:, 1, g * 512:(g + 1) * 512], ys[:, 1, g * 512:(g + 1) * 512], tmp, ALU.add)
            for t in range(T):
                dlink(dve, nc.vector.tensor_tensor(byhead(xst[:, t, :]), byhead(xst[:, t, :]), perhead(d_skip), ALU.mult))
                dlink(dve, nc.vector.tensor_tensor(ys[:, t, :], ys[:, t, :], xst[:, t, :], ALU.add))
                nc.vector.tensor_tensor(ys[:, t, :], ys[:, t, :], zs[:, t, :], ALU.mult)
            dve_end(dve)
            dve_end(dve)
            rstd_dve(dve, slice(4, 8))
            for t in range(T):
                for g in range(2):
                    i = 4 + 2 * t + g
                    nc.vector.tensor_scalar(ys[:, t, g * 512:(g + 1) * 512], ys[:, t, g * 512:(g + 1) * 512],
                                            stat[:, i:i + 1], None, ALU.mult)
            dve_end(dve)
            for k in range(12):
                b = next_d()
                if k < 4:
                    nc.vector.tensor_copy(mT[:, k, :], b[:, 0:S]).then_inc(dve_out, 1)
                else:
                    nc.vector.tensor_scalar(mT[:, k, :], b[:, 0:S], colA[:, 104 + k:105 + k], None, ALU.mult).then_inc(dve_out, 1)
            dve_end(dve)

        def wide8(o):
            return arena[:, o:o + 2048].rearrange("p (k n) -> p k n", k=KD)

        def bytok(a):
            return a.rearrange("p k n -> p (k n)").rearrange("p (t n) -> p t n", t=T)

        r_xx, r_x1, r_x2 = wide8(0), wide8(2048), wide8(4096)
        r_r, r_k, r_v, r_ld, r_a, r_g = (wide8(6144 + 2048 * i) for i in range(6))
        hflat = hT[:, :, :].rearrange("p k n -> p (k n)")[:, 0:2048]
        h8 = hflat.rearrange("p (k n) -> p k n", k=KD)
        ry = hflat.rearrange("p (t n) -> p t n", t=T)
        vtk, gtk = bytok(r_v), bytok(r_g)
        bonus = small[:, 384:416].rearrange("p (t h) -> p t h", t=T)
        mid = small[:, 416:432].rearrange("p (k t) -> p k t", t=T)
        emid, eend = small[:, 432:440], small[:, 440:448]
        gnm = arena[:, 18432:18464].rearrange("p (t h) -> p t h", t=T)
        gnv = arena[:, 18464:18496].rearrange("p (t h) -> p t h", t=T)
        sgT, sgT2 = arena[:, 2048:2304], arena[0:32, 2304:2560]
        th, al = arena[0:64, 16384:16640], arena[0:64, 16640:16896]
        TTs = arena[:, 0:2048].rearrange("p (h n) -> p h n", h=SH)
        q4 = lambda o: [arena[:, o + 512 * b:o + 512 * b + 512].rearrange("p (h n) -> p h n", h=4) for b in range(2)]
        iT, iM, iAT, iL = q4(4096), q4(5120), q4(12288), q4(13312)
        bend = arena[:, 4096:6144].rearrange("p (w n) -> p w n", w=2)
        btk, ktk = gains[:, 0, :], gains[:, 1, :]
        s0bd = gains[:, 11, :].rearrange("p (j n) -> p j n", j=KD)
        gA = [arena[:, 4096 + 768 * b:4096 + 768 * (b + 1)] if b < 2 else arena[:, 12288 + 768 * (b - 2):12288 + 768 * (b - 1)]
              for b in range(4)]
        gA = [g.rearrange("p (h w n) -> p h w n", h=2, w=3) for g in gA]
        rhs_sb = [arena[:, 5632 + P * b:5632 + P * (b + 1)] for b in range(4)]
        u_sb = [arena[:, 13824 + P * b:13824 + P * (b + 1)] for b in range(4)]
        mix_ready, mix_used, level_ready = sem("mix_ready"), sem("mix_used"), sem("level_ready")
        MU = [0, 2, 3, 1, 4, 5]
        XB = [r_x1, r_x2]
        lvl_pe = Turn()
        chunk_base = []

        def rwkv_pe(pe):
            s = at["rwkv"]

            def wait_a(n):
                if n > 4:
                    pe.wait_ge(act_out, n - 4)

            def wait_d(n):
                if n > 4:
                    pe.wait_ge(dve_out, n - 4)

            for i in range(2):
                pe.wait_ge(mix_ready, i + 1)
                for k in range(KD):
                    if k % 2 == 0:
                        take_slot(pe, s)
                    n = pe_a()
                    wait_a(n)
                    group(bank_a(n)[:, 0:S], [(slot8(s)[:, c, (k % 2) * P:(k % 2 + 1) * P], XB[i][:, c, :]) for c in range(KD)])\
                        .then_inc(to_act, 1)
                    if k % 2 == 1:
                        pe.drain().then_inc(slot_used, 1)
                        s += 1
                pe.drain().then_inc(mix_used, 1)
            pe.wait_ge(mix_ready, 3)
            for c4 in range(4):
                take_slot(pe, s)
                n = pe_a()
                wait_a(n)
                for t in range(T):
                    m = group(bank_a(n)[:, t * 256:(t + 1) * 256],
                              [(r_x1[:, c, t * P:(t + 1) * P], slot8(s)[:, c, :]) for c in range(KD)])
                m.then_inc(to_act, 1)
                pe.drain().then_inc(slot_used, 1)
                s += 1
            pe.drain().then_inc(mix_used, 1)
            take_slot(pe, s)
            for i in range(2):
                pe.wait_ge(mix_ready, 4 + i)
                w1 = ring[:, s % NSLOT, 512 * i:512 * (i + 1)].rearrange("p (k n) -> p k n", k=KD)
                n = pe_a()
                wait_a(n)
                group(bank_a(n)[0:64, 0:S], [(w1[:, c, :], XB[1 - i][:, c, :]) for c in range(KD)]).then_inc(to_act, 1)
                pe.drain().then_inc(mix_used, 1)
            n_al = n
            pe.drain().then_inc(slot_used, 1)
            s += 1
            take_slot(pe, s)
            pe.wait_ge(act_out, n_al)
            for i in range(2):
                for k in range(KD):
                    n = pe_a()
                    wait_a(n)
                    group(bank_a(n)[:, 0:S], [(slot2(s)[0:64, i, k * P:(k + 1) * P], (th, al)[i])]).then_inc(to_act, 1)
            pe.drain().then_inc(slot_used, 1)
            s += 1
            take_slot(pe, s)
            pe.wait_ge(mix_ready, 6)
            g1 = ring[:, s % NSLOT, 0:KD * 160].rearrange("p (k n) -> p k n", k=KD)
            n = pe_a()
            wait_a(n)
            group(bank_a(n)[:, 0:S], [(g1[:, c, 0:P], r_x2[:, c, :]) for c in range(KD)])
            group(bank_a(n)[0:32, S:2 * S], [(g1[:, c, P:160], r_x2[:, c, :]) for c in range(KD)]).then_inc(to_act, 1)
            n_sg = n
            pe.drain().then_inc(slot_used, 1)
            s += 1
            take_slot(pe, s)
            pe.wait_ge(act_out, n_sg)
            for t in range(T):
                for h in range(2):
                    n = pe_a()
                    wait_a(n)
                    group(bank_a(n), [(sgT[:, t * P:(t + 1) * P], slot2(s)[:, 0, h * 512:(h + 1) * 512]),
                                      (sgT2[:, t * P:(t + 1) * P], slot2(s)[0:32, 1, h * 512:(h + 1) * 512])]).then_inc(to_act, 1)
            pe.drain().then_inc(slot_used, 1)
            pe_end(pe)
            pe_end(pe)
            for k in range(KD):
                n = pe_d()
                wait_d(n)
                group(bank_d(n)[:, 0:S], [(const("blockones"), r_x2[:, k, :])]).then_inc(to_dve, 1)
            pe_end(pe)
            pe_end(pe)
            pe_end(pe)
            n = pe_d()
            wait_d(n)
            for t in range(T):
                for k in range(KD):
                    m = group(bank_d(n)[:, t * 16 + 2 * k:t * 16 + 2 * k + 2], [(r_xx[:, k, t * P:(t + 1) * P], const("pairsel"))])
            m.then_inc(to_dve, 1)
            pe_end(pe)
            for t in range(T):
                invert_pe(pe, t, wait_d, wait_a)
                if t == 0:
                    pe_end(pe)
                    for w in range(2):
                        for j4 in range(2):
                            n = pe_a()
                            wait_a(n)
                            for j in range(4):
                                c = (4 * j4 + j) * P
                                m = nc.tensor.transpose(bank_a(n)[:, j * P:(j + 1) * P], bend[:, w, c:c + P], ident)
                            m.then_inc(to_act, 1)
                    pe_end(pe)
                chunk_pe(pe, t, wait_d, wait_a)
            pe_end(pe)
            pe_end(pe)
            pe_end(pe)
            for k in range(KD):
                n = pe_d()
                wait_d(n)
                for t in range(T):
                    m = nc.tensor.transpose(bank_d(n)[:, t * P:(t + 1) * P], ry[:, t, k * P:(k + 1) * P], ident)
                m.then_inc(to_dve, 1)
            pe_end(pe)
            product_pe(pe, at["rwkv_out"], KD, lambda k, t: r_xx[:, k, t * P:(t + 1) * P])

        def quad(q):
            return [(4 * (q // 2) + j, q % 2) for j in range(4)]

        def invert_pe(pe, t, wait_d, wait_a):
            tk = slice(t * P, (t + 1) * P)
            for q0 in (0, 2):
                for b in range(2):
                    for which in range(2):
                        n = pe_d()
                        wait_d(n)
                        for i, (j, hh) in enumerate(quad(q0 + b)):
                            hs = slice(hh * 64, hh * 64 + 64)
                            l, r = (r_a, r_x1) if which == 0 else (r_x1, r_a)
                            m = group(bank_d(n)[:, i * P:(i + 1) * P], [(l[hs, j, tk], r[hs, j, tk])])
                        m.then_inc(to_dve, 1)
                for lv in range(1, 7):
                    for b in range(2):
                        pe.wait_ge(level_ready, lvl_pe())
                        n = pe_a()
                        wait_a(n)
                        for i in range(4):
                            m = group(bank_a(n)[:, i * P:(i + 1) * P], [(iL[b][:, i, :], iT[b][:, i, :])])
                        m.then_inc(to_act, 1)
                    for b in range(2):
                        pe.wait_ge(act_out, pe_a.n - 1 + b)
                        TT = TTs[:, 4 * (q0 + b):4 * (q0 + b) + 4, :]
                        for which in range(2 if lv < 6 else 1):
                            n = pe_d()
                            wait_d(n)
                            for i in range(4):
                                pair = (iM[b][:, i, :], TT[:, i, :]) if which == 0 else (TT[:, i, :], iM[b][:, i, :])
                                m = group(bank_d(n)[:, i * P:(i + 1) * P], [pair])
                            m.then_inc(to_dve, 1)
            pe_end(pe)

        def invert_act(act, t):
            for q0 in (0, 2):
                for lv in range(1, 7):
                    for b in range(2):
                        n = act_a()
                        act.wait_ge(to_act, n)
                        nc.scalar.activation(iM[b], bank_a(n).rearrange("p (h n) -> p h n", h=4), ACT.Copy).then_inc(act_out, 1)
            act_end(act)

        def invert_dve(dve, t):
            def over4(a):
                return a.rearrange("p (o n) -> p o n", o=1).broadcast_to([P, 4, P])

            def bank4():
                n = dve_d()
                dve.wait_ge(to_dve, n)
                return bank_d(n).rearrange("p (h n) -> p h n", h=4)

            for q0 in (0, 2):
                for b in range(2):
                    TT = TTs[:, 4 * (q0 + b):4 * (q0 + b) + 4, :]
                    ps4 = bank4()
                    nc.vector.tensor_copy(iAT[b], ps4)
                    nc.vector.tensor_tensor(TT, ps4, over4(level[:, 0:P]), ALU.mult).then_inc(dve_out, 1)
                    nc.vector.tensor_tensor(iT[b], bank4(), over4(const("level1")), ALU.mult).then_inc(dve_out, 1)
                    dve.wait_ge(dve_out, dve_d.n)
                    nc.vector.tensor_tensor(TT, TT, over4(ident), ALU.add)
                    nc.vector.tensor_tensor(iT[b], iT[b], over4(ident), ALU.add)
                    nc.vector.tensor_tensor(iL[b], iAT[b], over4(level[:, P:2 * P]), ALU.mult).then_inc(level_ready, 1)
                for lv in range(1, 7):
                    for b in range(2):
                        TT = TTs[:, 4 * (q0 + b):4 * (q0 + b) + 4, :]
                        if lv < 6:
                            dve.wait_ge(to_dve, dve_d.n + 2)
                        nc.vector.tensor_tensor(TT, TT, bank4(), ALU.add).then_inc(dve_out, 1)
                        if lv < 6:
                            nc.vector.tensor_tensor(iT[b], iT[b], bank4(), ALU.add).then_inc(dve_out, 1)
                            nc.vector.tensor_tensor(iL[b], iAT[b], over4(level[:, (lv + 1) * P:(lv + 2) * P]),
                                                    ALU.mult).then_inc(level_ready, 1)
            dve_end(dve)

        def chunk_pe(pe, t, wait_d, wait_a):
            tk = slice(t * P, (t + 1) * P)
            n_g, n_rhs, n_u = {}, {}, {}
            chunk_base.append(pe_a.n)
            for i in range(KD + 3):
                if i < KD:
                    j = i
                    for hh in range(2):
                        hs = slice(hh * 64, hh * 64 + 64)
                        n = pe_d()
                        wait_d(n)
                        for w, (l, r) in enumerate(((r_k, r_r), (r_k, r_x1), (r_a, r_r))):
                            m = group(bank_d(n)[:, w * P:(w + 1) * P], [(l[hs, j, tk], r[hs, j, tk])])
                        m.then_inc(to_dve, 1)
                    n_g[j] = n
                if 1 <= i <= KD:
                    j = i - 1
                    pe.wait_ge(dve_out, n_g[j])
                    n = pe_a()
                    wait_a(n)
                    n_rhs[j] = n
                    if t == 1:
                        nc.tensor.matmul(bank_a(n)[:, 0:P], r_x1[:, j, tk], s0bd[:, j, :], start=True, stop=False,
                                         skip_group_check=True)
                    for hh in range(2):
                        m = nc.tensor.matmul(bank_a(n)[:, hh * 64:hh * 64 + 64], gA[j % 4][:, hh, 1, :],
                                             vtk[:, t, j * P + hh * 64:j * P + hh * 64 + 64], start=(t == 0), stop=True,
                                             skip_group_check=True)
                    m.then_inc(to_act, 1)
                if 2 <= i <= KD + 1:
                    j = i - 2
                    pe.wait_ge(act_out, n_rhs[j])
                    n = pe_a()
                    wait_a(n)
                    n_u[j] = n
                    for hh in range(2):
                        q = 2 * (j // 4) + hh
                        m = group(bank_a(n)[:, hh * 64:hh * 64 + 64], [(TTs[:, 4 * q + j % 4, :], rhs_sb[j % 4][:, hh * 64:hh * 64 + 64])])
                    m.then_inc(to_act, 1)
                if i >= 3:
                    j = i - 3
                    pe.wait_ge(act_out, n_u[j])
                    n = pe_a()
                    wait_a(n)
                    if t == 1:
                        nc.tensor.matmul(bank_a(n)[:, 0:P], r_r[:, j, tk], s0bd[:, j, :], start=True, stop=False,
                                         skip_group_check=True)
                    for hh in range(2):
                        o = bank_a(n)[:, hh * 64:hh * 64 + 64]
                        nc.tensor.matmul(o, gA[j % 4][:, hh, 0, :], vtk[:, t, j * P + hh * 64:j * P + hh * 64 + 64],
                                         start=(t == 0), stop=False, skip_group_check=True)
                        m = nc.tensor.matmul(o, gA[j % 4][:, hh, 2, :], u_sb[j % 4][:, hh * 64:hh * 64 + 64],
                                             start=False, stop=True, skip_group_check=True)
                    m.then_inc(to_act, 1)
                    if t == 0:
                        n = pe_d()
                        wait_d(n)
                        group(bank_d(n)[:, 0:P], [(btk[:, j * P:(j + 1) * P], u_sb[j % 4]),
                                                  (ktk[:, j * P:(j + 1) * P], vtk[:, 0, j * P:(j + 1) * P])]).then_inc(to_dve, 1)
            pe_end(pe)

        def chunk_act(act, t):
            def taken(dst, c=P):
                n = act_a()
                act.wait_ge(to_act, n)
                nc.scalar.activation(dst, bank_a(n)[:, 0:c], ACT.Copy).then_inc(act_out, 1)

            for i in range(KD + 3):
                if 1 <= i <= KD:
                    taken(rhs_sb[(i - 1) % 4])
                if 2 <= i <= KD + 1:
                    taken(u_sb[(i - 2) % 4])
                if i >= 3:
                    taken(ry[:, t, (i - 3) * P:(i - 2) * P])
            act_end(act)

        def chunk_dve(dve, t):
            mask3 = cst[:, CONST["upper"][0]:CONST["upper"][0] + 3 * P].rearrange("p (w n) -> p w n", w=3)
            for i in range(KD + 3):
                if i < KD:
                    for hh in range(2):
                        n = dve_d()
                        dve.wait_ge(to_dve, n)
                        if i >= 4:
                            dve.wait_ge(to_act, chunk_base[t] + 3 * (i - 4) + 6)
                        nc.vector.tensor_tensor(gA[i % 4][:, hh, :, :], bank_d(n)[:, 0:3 * P].rearrange("p (w n) -> p w n", w=3),
                                                mask3, ALU.mult).then_inc(dve_out, 1)
                if i >= 3 and t == 0:
                    j = i - 3
                    n = dve_d()
                    dve.wait_ge(to_dve, n)
                    for hh in range(2):
                        hs = slice(hh * 64, hh * 64 + 64)
                        m = nc.vector.tensor_scalar(s0bd[hs, j, hs], bank_d(n)[hs, hs], emid[hs, j:j + 1], None, ALU.mult)
                    m.then_inc(dve_out, 1)
            dve_end(dve)

        def rwkv_act(act):
            def taken(dst, src, func=ACT.Copy, **kw):
                nc.scalar.activation(dst, src, func, **kw).then_inc(act_out, 1)

            def next_a():
                n = act_a()
                act.wait_ge(to_act, n)
                return bank_a(n)

            for i in range(2):
                for k in range(KD):
                    taken((r_r, r_k)[i][:, k, :], next_a()[:, 0:S])
            for c in range(4):
                taken(vtk[:, :, c * 256:(c + 1) * 256], next_a().rearrange("p (t n) -> p t n", t=T))
            taken(th, next_a()[0:64, 0:S], ACT.Tanh)
            taken(al, next_a()[0:64, 0:S])
            for i in range(2):
                for k in range(KD):
                    taken((r_ld, r_a)[i][:, k, :], next_a()[:, 0:S], ACT.Sigmoid, bias=colB[:, 48 + 8 * i + k:49 + 8 * i + k])
            b = next_a()
            nc.scalar.activation(sgT, b[:, 0:S], ACT.Sigmoid)
            taken(sgT2, b[0:32, S:2 * S], ACT.Sigmoid)
            for t in range(T):
                for h in range(2):
                    taken(gtk[:, t, h * 512:(h + 1) * 512], next_a())
            act_end(act)
            act_end(act)
            act_end(act)
            nc.scalar.activation(r_xx[:, :, :], r_xx[:, :, :], ACT.Sqrt)
            act_end(act)
            nc.scalar.activation(h8, r_x2[:, :, :], ACT.Exp, scale=-1.0)
            alink(act, nc.scalar.activation(emid, mid[:, :, 1], ACT.Exp))
            nc.scalar.activation(r_x2[:, :, :], r_x2[:, :, :], ACT.Exp)
            nc.scalar.activation(r_ld[:, :, :], r_ld[:, :, :], ACT.Exp)
            act_end(act)
            act_end(act)
            for t in range(T):
                invert_act(act, t)
                if t == 0:
                    act_end(act)
                    for w in range(2):
                        for j4 in range(2):
                            taken((btk, ktk)[w][:, j4 * 512:(j4 + 1) * 512], next_a())
                    act_end(act)
                chunk_act(act, t)
            act_end(act)
            nc.scalar.activation(gnv[:, :, :], gnv[:, :, :], ACT.Sqrt, scale=1.0 / 64, bias=const("eps")[:, 2:3])
            act_end(act)
            act_end(act)
            act_end(act)
            act_end(act)

        def rwkv_dve(dve):
            hk = hT[:, :, META:]
            nc.vector.tensor_tensor(r_xx[:, :, 1:], hk[:, :, 0:S - 1], hk[:, :, 1:], ALU.subtract)
            dlink(dve, nc.vector.tensor_scalar(r_xx[:, :, 0:1], hk[:, :, 0:1], -1.0, None, ALU.mult))
            for i in range(6):
                if i >= 2:
                    dve.wait_ge(mix_used, i - 1)
                for k in range(KD):
                    c = 8 * MU[i] + k
                    m = nc.vector.scalar_tensor_tensor(XB[i % 2][:, k, :], r_xx[:, k, :], colB[:, c:c + 1], hk[:, k, :],
                                                       ALU.mult, ALU.add)
                m.then_inc(mix_ready, 1)
            dve_end(dve)
            col = lambda o, k: colB[:, o + k:o + k + 1]
            nc.vector.tensor_scalar(r_ld[:, :, :], r_ld[:, :, :], -float(np.exp(-0.5)), None, ALU.mult)
            for k in range(KD):
                nc.vector.tensor_scalar(r_x1[:, k, :], r_k[:, k, :], col(64, k), None, ALU.mult)
                m = nc.vector.tensor_scalar(r_xx[:, k, :], r_a[:, k, :], -1.0, col(72, k), ALU.add, ALU.mult)
            dlink(dve, m)
            nc.vector.tensor_tensor(r_x2[:, :, :], r_x1[:, :, :], r_x1[:, :, :], ALU.mult)
            nc.vector.scalar_tensor_tensor(r_k[:, :, :], r_xx[:, :, :], 1.0, r_k[:, :, :], ALU.add, ALU.mult)
            dve_end(dve)
            for k in range(KD):
                n = dve_d()
                dve.wait_ge(to_dve, n)
                nc.vector.tensor_scalar(r_xx[:, k, :], bank_d(n)[:, 0:S], 1e-24, None, ALU.max).then_inc(dve_out, 1)
            dve_end(dve)
            for k in range(KD):
                for t in range(T):
                    tk = slice(t * P, (t + 1) * P)
                    m = nc.vector.tensor_tensor_scan(r_x2[:, k, tk], ones, r_ld[:, k, tk], 0.0, ALU.mult, ALU.add)
            dlink(dve, m)
            c4 = r_x2[:, :, :].rearrange("p k (t n) -> p k t n", t=T)
            dlink(dve, nc.vector.tensor_copy(mid, c4[:, :, :, 63]))
            for t in range(T):
                dlink(dve, nc.vector.tensor_tensor(c4[:, :, t, :], c4[:, :, t, :],
                                                   mid[:, :, t:t + 1].broadcast_to([P, KD, P]), ALU.subtract))
            nc.vector.tensor_tensor(r_ld[:, :, :], r_x2[:, :, :], r_ld[:, :, :], ALU.subtract)
            dve_end(dve)
            dlink(dve, nc.vector.reciprocal(r_xx[:, :, :], r_xx[:, :, :]))
            dlink(dve, nc.vector.tensor_tensor(r_x1[:, :, :], r_x1[:, :, :], r_xx[:, :, :], ALU.mult))
            for k in range(KD):
                nc.vector.scalar_tensor_tensor(r_xx[:, k, :], r_r[:, k, :], col(80, k), r_k[:, k, :], ALU.mult, ALU.mult)
            dve_end(dve)
            nc.vector.tensor_copy(eend, r_x2[:, :, P - 1])
            nc.vector.tensor_tensor(r_r[:, :, :], r_r[:, :, :], r_x2[:, :, :], ALU.mult)
            nc.vector.tensor_tensor(r_k[:, :, :], r_k[:, :, :], h8, ALU.mult)
            dlink(dve, nc.vector.tensor_tensor(r_a[:, :, :], r_a[:, :, :], r_x1[:, :, :], ALU.mult))
            nc.vector.tensor_tensor(r_a[:, :, :], r_a[:, :, :], h8, ALU.mult)
            nc.vector.scalar_tensor_tensor(r_x1[:, :, :], r_x1[:, :, :], -1.0, r_ld[:, :, :], ALU.mult, ALU.mult)
            nc.vector.memset(s0bd[:, :, :], 0.0)
            n = dve_d()
            dve.wait_ge(to_dve, n)
            nc.vector.tensor_copy(bonus, bank_d(n)[:, 0:32].rearrange("p (t h) -> p t h", t=T)).then_inc(dve_out, 1)
            dve_end(dve)
            for t in range(T):
                invert_dve(dve, t)
                if t == 0:
                    for w in range(2):
                        for k in range(KD):
                            nc.vector.tensor_scalar(bend[:, w, k * P:(k + 1) * P], (r_a, r_k)[w][:, k, 0:P], eend[:, k:k + 1],
                                                    None, ALU.mult)
                    dve_end(dve)
                    dve_end(dve)
                chunk_dve(dve, t)
            bh = lambda a: a.rearrange("p (h n) -> p h n", n=64)
            ph = lambda a: a.rearrange("p (h o) -> p h o", o=1).broadcast_to([P, SH, 64])
            sq = bytok(r_x2)
            for t in range(T):
                m = nc.vector.tensor_reduce(gnm[:, t, :], bh(ry[:, t, :]), AX, ALU.add)
            dlink(dve, m)
            dlink(dve, nc.vector.tensor_scalar(gnm[:, :, :], gnm[:, :, :], 1.0 / 64, None, ALU.mult))
            for t in range(T):
                dlink(dve, nc.vector.tensor_tensor(bh(ry[:, t, :]), bh(ry[:, t, :]), ph(gnm[:, t, :]), ALU.subtract))
                dlink(dve, nc.vector.tensor_tensor(sq[:, t, :], ry[:, t, :], ry[:, t, :], ALU.mult))
                nc.vector.tensor_reduce(gnv[:, t, :], bh(sq[:, t, :]), AX, ALU.add)
            dve_end(dve)
            for t in range(T):
                nc.vector.tensor_tensor(bh(vtk[:, t, :]), bh(vtk[:, t, :]), ph(bonus[:, t, :]), ALU.mult)
            dve_end(dve)
            dlink(dve, nc.vector.reciprocal(gnv[:, :, :], gnv[:, :, :]))
            for t in range(T):
                y = ry[:, t, :]
                dlink(dve, nc.vector.tensor_tensor(bh(y), bh(y), ph(gnv[:, t, :]), ALU.mult))
                dlink(dve, nc.vector.tensor_tensor(y, y, gains[:, LN_G, :], ALU.mult))
                dlink(dve, nc.vector.tensor_tensor(y, y, gains[:, LN_B, :], ALU.add))
                dlink(dve, nc.vector.tensor_tensor(y, y, vtk[:, t, :], ALU.add))
                nc.vector.tensor_tensor(y, y, gtk[:, t, :], ALU.mult)
            dve_end(dve)
            for k in range(KD):
                n = dve_d()
                dve.wait_ge(to_dve, n)
                nc.vector.tensor_copy(r_xx[:, k, :], bank_d(n)[:, 0:S]).then_inc(dve_out, 1)
            dve_end(dve)
            dve_end(dve)

        fmh = arena[:, 0:16 * L2].rearrange("p (i n) -> p i n", i=16)
        tokh = arena[:, 4352:8448].rearrange("p (w t n) -> p w t n", w=4, t=T)
        tokm = arena[0:META, 8448:10496].rearrange("p (w n) -> p w n", w=4)
        oh = arena[:, 10496:12544].rearrange("p (t n) -> p t n", t=T)
        om = arena[0:META, 12544:13568]
        fl = arena[0:8, 13568:13840]
        fl2 = arena[0:8, 13840:14112]
        osq = arena[:, 14200:15224].rearrange("p (t n) -> p t n", t=T)
        osm = arena[0:META, 15224:15736]
        hmT = arena[:, 0:KD * L2].rearrange("p (k n) -> p k n", k=KD)
        hst = small[:, 448:480]
        nlam = small[:, 96:97]
        rth = arena[:, 14200:14744].rearrange("p (b n) -> p b n", b=2)

        def units(layer):
            tiles = ([T] if layer == 0 else []) + list(range(T))
            return [(t, kind, h) for t in tiles for kind, nh in (("diff", 4), ("fox", 8)) for h in range(nh)]

        def u_rows(u):
            return META if u[0] == T else P

        def u_width(u):
            return META if u[0] == T else META + (u[0] + 1) * P

        def u_keys(u):
            return [(None, 0, META, 0)] + [(k, META + k * P, P, (k + 1) * P) for k in range(0 if u[0] == T else u[0] + 1)]

        def u_comps(u):
            return 2 if u[1] == "diff" else 1

        def hybrid_pe(pe, layer):
            s = at[("hybrid", layer)]

            def wait_a(n):
                if n > 4:
                    pe.wait_ge(act_out, n - 4)

            def wait_d(n):
                if n > 4:
                    pe.wait_ge(dve_out, n - 4)

            for part in range(8):
                for half in range(2):
                    take_slot(pe, s)
                    if part in (0, 1, 4, 5):
                        for c in range(2):
                            n = pe_d()
                            wait_d(n)
                            group(bank_d(n)[:, 0:L2], [(slot8(s)[:, k, c * P:(c + 1) * P], hT[:, k, :]) for k in range(KD)])\
                                .then_inc(to_dve, 1)
                    else:
                        n = pe_a()
                        wait_a(n)
                        for t in range(T):
                            m = group(bank_a(n)[:, t * 256:(t + 1) * 256],
                                      [(hT[:, k, META + t * P:META + (t + 1) * P], slot8(s)[:, k, :]) for k in range(KD)])
                        m.then_inc(to_act, 1)
                        if layer == 0 or part in (2, 6):
                            n = pe_a()
                            wait_a(n)
                            group(bank_a(n)[0:META, 0:256], [(hT[:, k, 0:META], slot8(s)[:, k, :]) for k in range(KD)])\
                                .then_inc(to_act, 1)
                    pe.drain().then_inc(slot_used, 1)
                    s += 1
            take_slot(pe, s)
            n = pe_d()
            wait_d(n)
            group(bank_d(n)[0:8, 0:L2], [(slot8(s, 8)[:, k, :], hT[:, k, :]) for k in range(KD)]).then_inc(to_dve, 1)
            pe.drain().then_inc(slot_used, 1)
            pe_end(pe)
            for i in range(8):
                n = pe_d()
                wait_d(n)
                group(bank_d(n)[:, 0:L2], [(const("rot"), fmh[:, i, :])]).then_inc(to_dve, 1)
            pe_end(pe)
            pe_end(pe)

            def q_cols(t):
                return slice(0, META) if t == T else slice(META + t * P, META + (t + 1) * P)

            def scores(u, c, bank):
                t, kind, h = u
                if c >= u_comps(u):
                    return []
                r, w = u_rows(u), u_width(u)
                if kind == "diff":
                    hs = slice(c * 64, c * 64 + 64)
                    return [(bank[0:r, 0:w], [(fmh[hs, h, q_cols(t)], fmh[hs, 4 + h, 0:w])])]
                hs = slice((h % 2) * 64, (h % 2) * 64 + 64)
                return [(bank[0:r, 0:w], [(fmh[hs, 8 + h // 2, q_cols(t)], fmh[hs, 12 + h // 2, 0:w]),
                                          (ident[0:8, h:h + 1].broadcast_to([8, r]), fl[:, 0:w])])]

            def blocks(u, b):
                r = u_rows(u)
                return [(prob[0:r, b, 0, k0:k0 + n], r, n, col) for _, k0, n, col in u_keys(u)]

            def values(u, b, bank):
                t, kind, h = u
                r = u_rows(u)
                w, cols = (0, slice(h * P, (h + 1) * P)) if kind == "diff" else (2, slice(h * 64, (h + 1) * 64))
                pairs = [(probT[0:n, b, col:col + r], tokm[:, w, cols] if k is None else tokh[:, w, k, cols])
                         for k, _, n, col in u_keys(u)]
                return bank[0:r, 0:cols.stop - cols.start], pairs

            attend_pe(pe, units(layer), scores, blocks, values)
            pe_end(pe)
            pe_end(pe)
            pe_end(pe)
            for k in range(KD):
                n = pe_d()
                wait_d(n)
                if layer == 0:
                    nc.tensor.transpose(bank_d(n)[:, 0:META], om[:, k * P:(k + 1) * P], ident[0:META, 0:META])
                for t in range(T):
                    m = nc.tensor.transpose(bank_d(n)[:, META + t * P:META + (t + 1) * P], oh[:, t, k * P:(k + 1) * P], ident)
                m.then_inc(to_dve, 1)
            pe_end(pe)
            product_pe(pe, at[("hybrid_out", layer)], KD, lambda k, t: hmT[:, k, q_cols(t)], meta=layer == 0)
            pe_end(pe)

        def hybrid_act(act, layer):
            for part in (2, 3, 6, 7):
                w = (part // 4) * 2 + part % 2
                f = ACT.Silu if part % 2 else ACT.Copy
                for half in range(2):
                    n = act_a()
                    act.wait_ge(to_act, n)
                    nc.scalar.activation(tokh[:, w, :, half * 256:(half + 1) * 256],
                                         bank_a(n).rearrange("p (t n) -> p t n", t=T), f).then_inc(act_out, 1)
                    if layer == 0 or part in (2, 6):
                        n = act_a()
                        act.wait_ge(to_act, n)
                        nc.scalar.activation(tokm[:, w, half * 256:(half + 1) * 256], bank_a(n)[0:META, 0:256], f)\
                            .then_inc(act_out, 1)
            act_end(act)
            alink(act, nc.scalar.activation(fl2, fl, ACT.Abs))
            alink(act, nc.scalar.activation(fl2, fl2, ACT.Exp, scale=-1.0))
            nc.scalar.activation(fl2, fl2, ACT.Ln, bias=1.0)
            nc.scalar.activation(lam[:, 1:3], lam[:, 1:3], ACT.Exp)
            act_end(act)
            act_end(act)
            attend_act(act, units(layer), u_rows, u_width,
                       lambda u: [(n, col, col + u_rows(u)) for _, _, n, col in u_keys(u)], u_comps)
            act_end(act)
            nc.scalar.activation(hst[:, 0:8], hst[:, 0:8], ACT.Sqrt, scale=1.0 / P, bias=const("eps")[:, 0:1])
            if layer == 0:
                nc.scalar.activation(hst[0:META, 8:12], hst[0:META, 8:12], ACT.Sqrt, scale=1.0 / P,
                                     bias=const("eps", META)[:, 0:1])
            act_end(act)
            act_end(act)
            act_end(act)
            act_end(act)
            act_end(act)

        def hybrid_dve(dve, layer):
            l_init = 0.8 - 0.6 * float(np.exp(-0.3 * layer))

            def next_d():
                n = dve_d()
                dve.wait_ge(to_dve, n)
                return bank_d(n)

            lv = lambda i: gains[:, LAMB, (4 * layer + i) * 64:(4 * layer + i + 1) * 64]
            for i in range(2):
                dlink(dve, nc.vector.tensor_tensor(arena[:, 14200:14264], lv(2 * i), lv(2 * i + 1), ALU.mult))
                dlink(dve, nc.vector.tensor_reduce(lam[:, 1 + i:2 + i], arena[:, 14200:14264], AX, ALU.add))
            for i in range(16):
                if 8 <= i < 12:
                    nc.vector.tensor_scalar(fmh[:, i, :], next_d()[:, 0:L2], SCR, None, ALU.mult).then_inc(dve_out, 1)
                else:
                    nc.vector.tensor_copy(fmh[:, i, :], next_d()[:, 0:L2]).then_inc(dve_out, 1)
            nc.vector.tensor_scalar(fl, next_d()[0:8, 0:L2], forget[:, layer:layer + 1], None, ALU.add).then_inc(dve_out, 1)
            dve_end(dve)
            for i in range(8):
                b = next_d()
                tmp, raw = rth[:, i % 2, :], fmh[:, i, :]
                nc.vector.tensor_tensor(tmp, b[:, 0:L2], const("sin"), ALU.mult).then_inc(dve_out, 1)
                dlink(dve, nc.vector.tensor_tensor(raw, raw, const("cos"), ALU.mult))
                dlink(dve, nc.vector.tensor_tensor(raw, raw, tmp, ALU.add))
                if i < 4:
                    nc.vector.tensor_scalar(raw, raw, SCR, None, ALU.mult)
            dve_end(dve)
            dlink(dve, nc.vector.scalar_tensor_tensor(fl2, fl, 0.0, fl2, ALU.min, ALU.subtract))
            dlink(dve, nc.vector.tensor_tensor_scan(fl, ones[0:8, 0:1].broadcast_to([8, L2]), fl2, 0.0, ALU.mult, ALU.subtract))
            dlink(dve, nc.vector.tensor_scalar(nlam, lam[:, 2:3], -l_init, None, ALU.add))
            dlink(dve, nc.vector.tensor_tensor(nlam, nlam, lam[:, 1:2], ALU.subtract))
            dve_end(dve)

            def mask(u):
                if u[0] == T:
                    return qmask[0:META, L2 - P:L2 - P + META]
                return qmask[:, L2 - u_width(u):]

            def combine(dve, u, b):
                r, w = u_rows(u), u_width(u)
                p0, p1 = prob[0:r, b, 0, 0:w], prob[0:r, b, 1, 0:w]
                first = nc.vector.tensor_scalar(p0, p0, astat[0:r, b, 4:5], None, ALU.mult)
                if u[1] == "fox":
                    return first
                dlink(dve, first)
                dlink(dve, nc.vector.tensor_tensor(astat[0:r, b, 5:6], astat[0:r, b, 5:6], nlam[0:r], ALU.mult))
                return nc.vector.scalar_tensor_tensor(p0, p1, astat[0:r, b, 5:6], p0, ALU.mult, ALU.add)

            def take(dve, u, b, bank):
                t, kind, h = u
                r = u_rows(u)
                c0, n = (h * P, P) if kind == "diff" else (512 + h * 64, 64)
                dst = om[:, c0:c0 + n] if t == T else oh[:, t, c0:c0 + n]
                return nc.vector.tensor_copy(dst, bank[0:r, 0:n])

            attend_dve(dve, units(layer), u_rows, u_width, mask, combine, take, u_comps)
            heads = lambda a: a.rearrange("p (h n) -> p h n", h=4)
            per = lambda a: a.rearrange("p (h o) -> p h o", o=1).broadcast_to([a.shape[0], 4, P])
            rows = [(oh[:, t, :], osq[:, t, :], hst[:, 4 * t:4 * t + 4], P, t) for t in range(T)]
            if layer == 0:
                rows.append((om, osm, hst[0:META, 8:12], META, T))
            for o, sq, ss, r, t in rows:
                dlink(dve, nc.vector.tensor_tensor(sq, o[:, 0:512], o[:, 0:512], ALU.mult))
                nc.vector.tensor_reduce(ss, heads(sq), AX, ALU.add)
            dve_end(dve)
            dve_end(dve)
            g = gains[:, SUBLN, layer * 512:(layer + 1) * 512]
            for o, sq, ss, r, t in rows:
                dlink(dve, nc.vector.reciprocal(ss, ss))
                dlink(dve, nc.vector.tensor_scalar(ss, ss, 1.0 - l_init, None, ALU.mult))
                dlink(dve, nc.vector.tensor_tensor(heads(o[:, 0:512]), heads(o[:, 0:512]), per(ss), ALU.mult))
                dlink(dve, nc.vector.tensor_tensor(o[:, 0:512], o[:, 0:512], g[0:r], ALU.mult))
                for w in range(2):
                    z = tokm[:, 2 * w + 1, :] if t == T else tokh[:, 2 * w + 1, t, :]
                    nc.vector.tensor_tensor(o[:, w * 512:(w + 1) * 512], o[:, w * 512:(w + 1) * 512], z, ALU.mult)
            dve_end(dve)
            for k in range(KD):
                lo = 0 if layer == 0 else META
                nc.vector.tensor_copy(hmT[:, k, lo:], next_d()[:, lo:L2]).then_inc(dve_out, 1)
            dve_end(dve)
            dve_end(dve)
            for t in range(T):
                nc.vector.tensor_tensor(x[:, t, :], x[:, t, :], ps[:, 2 * t:2 * t + 2, :].rearrange("p a b -> p (a b)"), ALU.add)
            if layer == 0:
                nc.vector.tensor_tensor(xm[:, :], xm[:, :], ps[0:META, 4:6, :].rearrange("p a b -> p (a b)"), ALU.add)
            dve_end(dve)

        block = ctx.enter_context(nc.Block())

        @block.scalar
        def _(act):
            first_loads(nc.scalar)

        @block.gpsimd
        def _(pool):
            pool.wait_ge(slot_used, NSLOT)
            later_loads(nc.gpsimd)

        @block.tensor
        def _(pe):
            prep_pe(pe)
            for layer in range(2):
                norm_pe(pe)
                ffn_pe(pe, 2 * layer)
                if layer == 0:
                    pe.wait_ge(later_in, 16 * n_later.n)
                resid_pe(pe)
                if stop == "ffn":
                    return
                norm_pe(pe)
                if layer == 0:
                    mixer_pe(pe)
                else:
                    rwkv_pe(pe)
                resid_pe(pe)
                if stop == ("mixer", "rwkv")[layer]:
                    return
                norm_pe(pe)
                ffn_pe(pe, 2 * layer + 1)
                resid_pe(pe)
            for layer in range(2):
                norm_pe(pe, meta=True)
                hybrid_pe(pe, layer)
            norm_pe(pe, last=True)
            pe_end(pe)

        @block.scalar
        def _(act):
            prep_act(act)
            for layer in range(2):
                c = 24 * layer
                norm_act(act, colA[:, c:c + 8])
                ffn_act(act, 2 * layer)
                if layer == 0:
                    act.wait_ge(later_in, 16 * n_later.n)
                resid_act(act)
                if stop == "ffn":
                    return
                norm_act(act, colA[:, c + 8:c + 16])
                if layer == 0:
                    mixer_act(act)
                else:
                    rwkv_act(act)
                resid_act(act)
                if stop == ("mixer", "rwkv")[layer]:
                    return
                norm_act(act, colA[:, c + 16:c + 24])
                ffn_act(act, 2 * layer + 1)
                resid_act(act)
            for layer in range(2):
                norm_act(act, colB[:, 88 + 8 * layer:96 + 8 * layer], meta=True)
                hybrid_act(act, layer)
            norm_act(act, None)
            act_end(act)

        @block.vector
        def _(dve):
            prep_dve(dve)
            for layer in range(2):
                c = 24 * layer
                norm_dve(dve, colA[:, c:c + 8])
                ffn_dve(dve, 2 * layer)
                if layer == 0:
                    dve.wait_ge(later_in, 16 * n_later.n)
                resid_dve(dve, 3 * layer, 0.5)
                if stop == "ffn":
                    return
                norm_dve(dve, colA[:, c + 8:c + 16])
                if layer == 0:
                    mixer_dve(dve)
                else:
                    rwkv_dve(dve)
                resid_dve(dve, 3 * layer + 1, 1.0)
                if stop == ("mixer", "rwkv")[layer]:
                    return
                norm_dve(dve, colA[:, c + 16:c + 24])
                ffn_dve(dve, 2 * layer + 1)
                resid_dve(dve, 3 * layer + 2, 0.5)
            for layer in range(2):
                norm_dve(dve, colB[:, 88 + 8 * layer:96 + 8 * layer], meta=True)
                hybrid_dve(dve, layer)
            norm_dve(dve, None)
            for t in range(T):
                nc.vector.tensor_tensor(xn[:, t, :], xn[:, t, :], gains[:, FINAL_G, :], ALU.mult)
            dve_end(dve)

        @block.sync
        def _(sp):
            for layer in range(2):
                load_ffn(sp, 2 * layer, d["ffn1_w_gate"][layer], d["ffn1_w_up"][layer], d["ffn1_w_down"][layer])
                if stop == "ffn":
                    break
                for n in range(at["mixer"] if layer == 0 else at["rwkv"], at[("ffn", 2 * layer + 1)]):
                    load_slot(sp, n)
                if stop == ("mixer", "rwkv")[layer]:
                    break
                load_ffn(sp, 2 * layer + 1, d["ffn2_w_gate"][layer], d["ffn2_w_up"][layer], d["ffn2_w_down"][layer])
            if stop is None:
                for n in range(at[("hybrid", 0)], len(plan)):
                    load_slot(sp, n)
            sp.wait_ge(stage_done, 3 * pe_sync.n)
            for t in range(T):
                sp.dma_start(out[0, t * P:(t + 1) * P, :], xn[:, t, :] if stop is None else x[:, t, :]).then_inc(out_done, 16)
            sp.wait_ge(out_done, 16 * T)


_STOP = None


def kernel(**inputs):
    import concourse.bacc as _bacc
    from concourse.bass_utils import run_bass_kernel_spmd as _run

    nc = _bacc.Bacc("TRN2", target_bir_lowering=False, num_devices=1)
    arrays, aps = {}, {}
    for name, value in list(inputs.items()) + [("consts", constants())]:
        a = np.ascontiguousarray(value)
        arrays[f"in_{name}"] = a
        aps[name] = nc.dram_tensor(f"in_{name}", a.shape, mybir.dt.from_np(a.dtype), kind="ExternalInput").ap()
    out = nc.dram_tensor("out", (1, S, D), F32, kind="ExternalOutput").ap()
    model_kernel(nc, aps, out, _STOP)
    return _run(nc, [arrays], core_ids=[0]).results[0]["out"]
```
